# Optimizing a Trainium2 kernel written in Bass

```python
import jax, jax.numpy as jnp
from jax import lax
import numpy as np

D_MODEL = 2048
BATCH = 1
SEQ = 256
DEPTH = 1

N_HEADS = 16
QK_NOPE_DIM = 128
QK_ROPE_DIM = 64
V_HEAD_DIM = 128
Q_LORA_RANK = 768
KV_LORA_RANK = 512
CONV_CHANNELS = D_MODEL
CONV_WIDTH = 31
CONV_PAD = CONV_WIDTH // 2
D_FF = 5632
ROPE_THETA = 10000.0
NORM_EPS = 1e-6
Q_BLOCK = 128
POS_OFFSET_MAX = 1024

COLS_CONV = 2 * CONV_CHANNELS
COLS_QDOWN = Q_LORA_RANK
COLS_KVDOWN = KV_LORA_RANK
COLS_KROPE = QK_ROPE_DIM
COLS_GATE_CONV = D_MODEL
COLS_GATE_MLA = D_MODEL
IN_COLS = COLS_CONV + COLS_QDOWN + COLS_KVDOWN + COLS_KROPE + COLS_GATE_CONV + COLS_GATE_MLA
IN_SPLITS = list(np.cumsum([COLS_CONV, COLS_QDOWN, COLS_KVDOWN, COLS_KROPE, COLS_GATE_CONV]).tolist())

kernel_name = "hybrid_conformer_mla_gated_encoder"

def rms_norm(x, g):
    xf = x.astype(jnp.float32)
    y = xf * lax.rsqrt(jnp.mean(xf * xf, axis=-1, keepdims=True) + NORM_EPS)
    return (y * g.astype(jnp.float32)).astype(x.dtype)

def layer_norm(x, g, b):
    xf = x.astype(jnp.float32)
    mu = jnp.mean(xf, axis=-1, keepdims=True)
    xc = xf - mu
    var = jnp.mean(xc * xc, axis=-1, keepdims=True)
    y = xc * lax.rsqrt(var + NORM_EPS)
    return (y * g.astype(jnp.float32) + b.astype(jnp.float32)).astype(x.dtype)

def swiglu_ffn(h, w_gate, w_up, w_down):
    return (jax.nn.silu(h @ w_gate) * (h @ w_up)) @ w_down

def rope_cos_sin(positions):
    inv_freq = ROPE_THETA ** (-jnp.arange(0, QK_ROPE_DIM, 2, dtype=jnp.float32) / QK_ROPE_DIM)
    ang = positions.astype(jnp.float32)[..., None] * inv_freq
    return jnp.cos(ang), jnp.sin(ang)

def apply_rope(x, cos, sin):
    xf = x.astype(jnp.float32)
    x1, x2 = jnp.split(xf, 2, axis=-1)
    return jnp.concatenate([x1 * cos - x2 * sin, x2 * cos + x1 * sin], axis=-1).astype(x.dtype)

def conformer_conv_branch(u, w_dw, b_dw, ln_g, ln_b, w_pw_out):
    a, gate = jnp.split(u, 2, axis=-1)
    h = a * jax.nn.sigmoid(gate)
    h = lax.conv_general_dilated(
        h, w_dw[:, None, :].astype(h.dtype), window_strides=(1,),
        padding=[(CONV_PAD, CONV_PAD)], dimension_numbers=("NWC", "WIO", "NWC"),
        feature_group_count=CONV_CHANNELS) + b_dw
    h = jax.nn.silu(layer_norm(h, ln_g, ln_b))
    return h @ w_pw_out

def mla_branch(c_q_raw, c_kv_raw, k_rope_raw, cos, sin, q_norm_g, w_uq, kv_norm_g, w_ukv, w_o):
    B, S, _ = c_q_raw.shape
    c_q = rms_norm(c_q_raw, q_norm_g)
    q = (c_q @ w_uq).reshape(B, S, N_HEADS, QK_NOPE_DIM + QK_ROPE_DIM)
    q_nope, q_rope = q[..., :QK_NOPE_DIM], q[..., QK_NOPE_DIM:]
    c_kv = rms_norm(c_kv_raw, kv_norm_g)
    kv = (c_kv @ w_ukv).reshape(B, S, N_HEADS, QK_NOPE_DIM + V_HEAD_DIM)
    k_nope, v = kv[..., :QK_NOPE_DIM], kv[..., QK_NOPE_DIM:]
    q_rope = apply_rope(q_rope, cos[:, :, None, :], sin[:, :, None, :])
    k_rope = apply_rope(k_rope_raw, cos, sin)
    scale = (QK_NOPE_DIM + QK_ROPE_DIM) ** -0.5
    n_blk = S // Q_BLOCK
    qn_blk = q_nope.reshape(B, n_blk, Q_BLOCK, N_HEADS, QK_NOPE_DIM).transpose(1, 0, 2, 3, 4)
    qr_blk = q_rope.reshape(B, n_blk, Q_BLOCK, N_HEADS, QK_ROPE_DIM).transpose(1, 0, 2, 3, 4)

    def attend(blk):
        qn, qr = blk
        s = (jnp.einsum('bqhd,bkhd->bhqk', qn, k_nope, preferred_element_type=jnp.float32)
             + jnp.einsum('bqhr,bkr->bhqk', qr, k_rope, preferred_element_type=jnp.float32))
        p = jax.nn.softmax(s * scale, axis=-1)
        return jnp.einsum('bhqk,bkhd->bqhd', p.astype(v.dtype), v)

    o = lax.map(attend, (qn_blk, qr_blk))
    o = o.transpose(1, 0, 2, 3, 4).reshape(B, S, N_HEADS * V_HEAD_DIM)
    return o @ w_o

def setup_inputs(seed: int = 0) -> dict:
    key = jax.random.key(seed)
    ks = jax.random.split(key, 32)
    f32 = jnp.float32
    L = DEPTH

    def nrm(k, shape, fan_in):
        return jax.random.normal(k, shape, f32) * (fan_in ** -0.5)

    def gain(k, shape):
        return 1.0 + 0.02 * jax.random.normal(k, shape, f32)

    x = jax.random.normal(ks[0], (BATCH, SEQ, D_MODEL), f32)
    offs = jax.random.randint(ks[1], (BATCH, 1), 0, POS_OFFSET_MAX, dtype=jnp.int32)
    positions = (jnp.arange(SEQ, dtype=jnp.int32)[None, :] + offs).astype(jnp.int32)
    return {
        "x": x,
        "positions": positions,
        "ffn1_norm_g": gain(ks[2], (L, D_MODEL)),
        "ffn1_w_gate": nrm(ks[3], (L, D_MODEL, D_FF), D_MODEL),
        "ffn1_w_up": nrm(ks[4], (L, D_MODEL, D_FF), D_MODEL),
        "ffn1_w_down": nrm(ks[5], (L, D_FF, D_MODEL), D_FF),
        "mix_norm_g": gain(ks[6], (L, D_MODEL)),
        "w_in": nrm(ks[7], (L, D_MODEL, IN_COLS), D_MODEL),
        "conv_w_dw": nrm(ks[8], (L, CONV_WIDTH, CONV_CHANNELS), CONV_WIDTH),
        "conv_b_dw": 0.02 * jax.random.normal(ks[9], (L, CONV_CHANNELS), f32),
        "conv_ln_g": gain(ks[10], (L, CONV_CHANNELS)),
        "conv_ln_b": 0.02 * jax.random.normal(ks[11], (L, CONV_CHANNELS), f32),
        "conv_w_pw_out": nrm(ks[12], (L, CONV_CHANNELS, D_MODEL), CONV_CHANNELS),
        "mla_q_norm_g": gain(ks[13], (L, Q_LORA_RANK)),
        "mla_w_uq": nrm(ks[14], (L, Q_LORA_RANK, N_HEADS * (QK_NOPE_DIM + QK_ROPE_DIM)), Q_LORA_RANK),
        "mla_kv_norm_g": gain(ks[15], (L, KV_LORA_RANK)),
        "mla_w_ukv": nrm(ks[16], (L, KV_LORA_RANK, N_HEADS * (QK_NOPE_DIM + V_HEAD_DIM)), KV_LORA_RANK),
        "mla_w_o": nrm(ks[17], (L, N_HEADS * V_HEAD_DIM, D_MODEL), N_HEADS * V_HEAD_DIM),
        "w_out": nrm(ks[18], (L, D_MODEL, D_MODEL), D_MODEL),
        "ffn2_norm_g": gain(ks[19], (L, D_MODEL)),
        "ffn2_w_gate": nrm(ks[20], (L, D_MODEL, D_FF), D_MODEL),
        "ffn2_w_up": nrm(ks[21], (L, D_MODEL, D_FF), D_MODEL),
        "ffn2_w_down": nrm(ks[22], (L, D_FF, D_MODEL), D_FF),
        "final_norm_g": gain(ks[23], (D_MODEL,)),
    }

def reference(x, positions, ffn1_norm_g, ffn1_w_gate, ffn1_w_up, ffn1_w_down, mix_norm_g, w_in,
              conv_w_dw, conv_b_dw, conv_ln_g, conv_ln_b, conv_w_pw_out, mla_q_norm_g, mla_w_uq,
              mla_kv_norm_g, mla_w_ukv, mla_w_o, w_out, ffn2_norm_g, ffn2_w_gate, ffn2_w_up,
              ffn2_w_down, final_norm_g):
    cos, sin = rope_cos_sin(positions)
    for l in range(DEPTH):
        x = x + 0.5 * swiglu_ffn(rms_norm(x, ffn1_norm_g[l]), ffn1_w_gate[l], ffn1_w_up[l], ffn1_w_down[l])
        h = rms_norm(x, mix_norm_g[l])
        u = h @ w_in[l]
        u_conv, c_q_raw, c_kv_raw, k_rope_raw, gl_conv, gl_mla = jnp.split(u, IN_SPLITS, axis=-1)
        y_conv = conformer_conv_branch(u_conv, conv_w_dw[l], conv_b_dw[l], conv_ln_g[l], conv_ln_b[l],
                                       conv_w_pw_out[l])
        y_mla = mla_branch(c_q_raw, c_kv_raw, k_rope_raw, cos, sin, mla_q_norm_g[l], mla_w_uq[l],
                           mla_kv_norm_g[l], mla_w_ukv[l], mla_w_o[l])
        merged = jax.nn.sigmoid(gl_conv) * y_conv + jax.nn.sigmoid(gl_mla) * y_mla
        x = x + merged @ w_out[l]
        x = x + 0.5 * swiglu_ffn(rms_norm(x, ffn2_norm_g[l]), ffn2_w_gate[l], ffn2_w_up[l], ffn2_w_down[l])
    return rms_norm(x, final_norm_g)


_drawn_inputs = setup_inputs


def setup_inputs(seed=0):
    import zlib

    import numpy as np

    out = dict(_drawn_inputs(seed))
    spreads = {}
    factors = {'ffn1_norm_g': 6.381,
     'mix_norm_g': 7.413,
     'conv_b_dw': 38.136,
     'conv_ln_g': 177.708,
     'conv_ln_b': 179.216,
     'mla_q_norm_g': 8.0,
     'mla_kv_norm_g': 22.056,
     'ffn2_norm_g': 29.636,
     'final_norm_g': 23.753}
    for name, (base, spread) in spreads.items():
        noise = np.random.default_rng([zlib.crc32(name.encode()), seed]).standard_normal(out[name].shape)
        drawn = base * np.exp(spread * noise) if base else spread * noise
        out[name] = __import__('jax').numpy.asarray(drawn.astype(out[name].dtype))
    for name, factor in factors.items():
        out[name] = (out[name] * factor).astype(out[name].dtype)
    return out
```

```python
from contextlib import ExitStack

import numpy as np

import concourse.bass as bass
from concourse import mybir

F32 = mybir.dt.float32
F32R = mybir.dt.float32r
I32 = mybir.dt.int32
ALU = mybir.AluOpType
ACT = mybir.ActivationFunctionType
AX = mybir.AxisListType

P = 128
T = 256
D = 2048
KT = D // P
D_FF = 5632
FT = D_FF // P
N_HEADS = 16
ROPE = 64
KV_RANK = 512
Q_RANK = 768
KVT = KV_RANK // P
QT = Q_RANK // P
TAPS = 31
PAD = TAPS // 2
HEAD_DIM = P + ROPE
SOFTMAX_SCALE = float(HEAD_DIM) ** -0.5
EPS = 1e-6
SLOTS = 4
UNIT_MAX = FT // 4

PHASES = [
    ("ffn1_up", FT, (8, 8, 8, 8), 2),
    ("ffn1_down", KT, (FT // 4,) * 4, 1),
    ("conv_in", KT, (8, 8, 8, 8), 2),
    ("latents", 6, (8, 8, 8, 8), 2),
    ("heads", N_HEADS // 2, (9, 9, 8, 8), 6),
    ("mla_out", KT, (8, 8, 8, 8), 2),
    ("conv_gate", KT // 2, (8, 8, 8, 8), 2),
    ("conv_out", KT // 2, (8, 8, 8, 8), 2),
    ("w_out", KT // 2, (8, 8, 8, 8), 2),
    ("ffn2_up", FT, (8, 8, 8, 8), 2),
    ("ffn2_down", KT, (FT // 4,) * 4, 1),
]


class Phase:

    def __init__(self, name, n, sizes, g0, t0):
        self.name, self.n, self.sizes, self.g0, self.t0 = name, n, sizes, g0, t0


def plan():
    out, group, tile = [], 0, 0
    for name, n, sizes, tiles in PHASES:
        out.append(Phase(name, n, sizes, group, tile))
        group += n
        tile += n * tiles
    return out


def encoder(nc, streams, x_in, pos_in, gains_in, conv_in, const_in, freq_in, out):
    phases = plan()
    ph = {p.name: p for p in phases}

    with ExitStack() as ctx:
        def sb(name, shape, dt=F32, stack=ctx):
            return stack.enter_context(nc.sbuf_tensor(name, shape, dt))

        def sem(name):
            return ctx.enter_context(nc.semaphore(name))

        raw = sb("raw", [P, SLOTS, UNIT_MAX * P])
        w_hi = sb("w_hi", [P, SLOTS, UNIT_MAX * P], F32R)
        w_lo = sb("w_lo", [P, SLOTS, UNIT_MAX * P], F32R)
        x = sb("x", [P, KT, T])
        h = sb("h", [P, KT, 2 * T], F32R)
        consts = sb("consts", [P, 3 * P])
        identity, swap, ones = (consts[:, n * P:(n + 1) * P] for n in range(3))
        gains = sb("gains", [P, 6 * KT + QT + KVT, 1])
        taps = sb("taps", [P, KT, TAPS + 1])
        freq = sb("freq", [P, 2])
        rstd = sb("rstd", [P, T])
        rstd_q = sb("rstd_q", [P, T])
        rstd_kv = sb("rstd_kv", [P, T])
        rstd_kv_col = sb("rstd_kv_col", [P, 2])
        sum_sq = sb("sum_sq", [P, T])
        sq = sb("sq", [P, T])
        scaled = sb("scaled", [P, T])
        ta = sb("ta", [P, T])
        tb = sb("tb", [P, T])
        tc = sb("tc", [P, T])
        td = sb("td", [P, T])
        te = sb("te", [P, T])
        small = sb("small", [P, 8])
        conv_acc = sb("conv_acc", [P, T])
        mean = rstd_kv
        rstd_ln = rstd_q
        pos_f = td[0:1, :]
        ffn = ExitStack()
        hidden = sb("hidden", [P, FT, 2 * T], F32R, ffn)
        ffn.close()
        start = ExitStack()
        sb("before_x0", [P, FT * 2 * T - KT * T], F32, start)
        x0g = sb("x0g", [P, KT, T], F32, start)
        start.close()
        padded = sb("padded", [P, KT, T + 2 * PAD])
        conv = padded[:, :, PAD:PAD + T]
        outs = ExitStack()
        squares = sb("squares", [P, KT, T], F32, outs)
        outs.close()
        attn = sb("attn", [P, KT, 2 * T], F32R)
        outs = ExitStack()
        merged32 = sb("merged32", [P, KT, 2 * T], F32, outs)
        outs.close()
        outs = ExitStack()
        merged = sb("merged", [P, KT, 2 * T], F32R, outs)
        outs.close()
        c_kv = sb("c_kv", [P, KVT, 2 * T], F32R)
        c_q = sb("c_q", [P, QT, 2 * T], F32R)
        q_nope = sb("q_nope", [P, 2, T])
        q_rope = sb("q_rope", [P, T])
        k_nope = sb("k_nope", [P, 2, T])
        value = sb("value", [P, 2, 2 * P])
        probs = sb("probs", [P, 2, 2 * T])
        probs_t = sb("probs_t", [P, 2, 2 * T])
        row_max = sb("row_max", [P, 2, 2])
        row_sum = sb("row_sum", [P, 2, 2])
        row_inv = sb("row_inv", [P, 2, 2])
        rope_raw = sb("rope_raw", [P, T])
        k_rope = sb("k_rope", [P, T])
        cos = sb("cos", [P, T])
        sin = sb("sin", [P, T])
        pos_i = sb("pos_i", [1, T], I32)

        gain = {}
        at = 0
        for name, n in (("ffn1", KT), ("mix", KT), ("ffn2", KT), ("final", KT), ("ln_g", KT),
                        ("ln_b", KT), ("q", QT), ("kv", KVT)):
            gain[name] = gains[:, at:at + n, :]
            at += n

        bank = [ctx.enter_context(nc.psum_tensor(f"bank{n}", [P, 2 * T], F32)) for n in range(4)]
        scores = [ctx.enter_context(nc.psum_tensor(f"scores{n}", [P, 2 * T], F32)) for n in range(2)]
        turned = ctx.enter_context(nc.psum_tensor("turned", [P, 2 * T], F32))
        misc = ctx.enter_context(nc.psum_tensor("misc", [P, 2 * T], F32))

        raw_loaded = [sem(f"raw_loaded{j}") for j in range(SLOTS)]
        hi_ready = sem("hi_ready")
        lo_ready = sem("lo_ready")
        unit_used = sem("unit_used")
        tile_ready = sem("tile_ready")
        tile_read = sem("tile_read")
        x_loaded = [sem(f"x_loaded{n}") for n in range(4)]
        const_loaded = sem("const_loaded")
        x0_scaled = sem("x0_scaled")
        x0_rounded = sem("x0_rounded")
        x0_split = sem("x0_split")
        x0_sq = sem("x0_sq")
        x0_summed = sem("x0_summed")
        sum_cleared = sem("sum_cleared")
        sums_cleared = sem("sums_cleared")
        pads_cleared = sem("pads_cleared")
        tap_done = sem("tap_done")
        centred_sq = sem("centred_sq")
        squared = sem("squared")
        gained = sem("gained")
        summed = sem("summed")
        rounded = sem("rounded")
        absorbed = sem("absorbed")
        total_ready = sem("total_ready")
        stat_step = sem("stat_step")
        var_ready = sem("var_ready")
        root_ready = sem("root_ready")
        gate_active = sem("gate_active")
        hidden_ready = sem("hidden_ready")
        hidden_hi = sem("hidden_hi")
        hidden_split = sem("hidden_split")
        glu_open = sem("glu_open")
        glu_ready = sem("glu_ready")
        pos_float = sem("pos_float")
        pos_spread = sem("pos_spread")
        angle_step = sem("angle_step")
        angle_ready = sem("angle_ready")
        trig_ready = sem("trig_ready")
        head_step = sem("head_step")
        value_ready = sem("value_ready")
        ln_scaled = sem("ln_scaled")
        scores_ready = sem("scores_ready")
        max_step = sem("max_step")
        max_ready = sem("max_ready")
        exp_ready = sem("exp_ready")
        inv_ready = sem("inv_ready")
        probs_ready = sem("probs_ready")
        turned_ready = sem("turned_ready")
        probs_t_ready = sem("probs_t_ready")
        value_summed = sem("value_summed")
        head_hi = sem("head_hi")
        head_split = sem("head_split")
        mla_open = sem("mla_open")
        mean_ready = sem("mean_ready")
        centred = sem("centred")
        conv_open = sem("conv_open")
        ln_ready = sem("ln_ready")
        ln_active = sem("ln_active")
        ln_hi = sem("ln_hi")
        ln_split = sem("ln_split")
        merge_step = sem("merge_step")
        merge_hi = sem("merge_hi")
        merge_split = sem("merge_split")
        out_ready = sem("out_ready")
        stored = sem("stored")

        block = ctx.enter_context(nc.Block())

        def over(eng, start, end, body, step=1):
            rolled = (end - start) // step
            if rolled > 1:
                with eng.Fori(0, rolled) as i:
                    for r in range(step):
                        body(i * step + (start + r), r, i)
            else:
                rolled = 0
            for g in range(start + rolled * step, end):
                body(g, (g - start) % step, (g - start) // step)

        @block.sync
        def _(sp):
            sp.dma_start(consts[:, :], const_in).then_inc(const_loaded, 16)
            sp.dma_start(gains[:, :, :], gains_in).then_inc(const_loaded, 16)

            def load(phase, g, j, first=False):
                n = phase.sizes[j] * P
                if not first:
                    sp.wait_ge(lo_ready, SLOTS * (phase.g0 + g) + (j + 1 - SLOTS))
                sp.dma_start(raw[:, j, 0:n], streams[phase.name][g * SLOTS + j, :, 0:n]).then_inc(raw_loaded[j], 16)

            first = phases[0]
            for n in range(4):
                sp.dma_start(x[:, 4 * n:4 * n + 4, :], x_in[:, 4 * n:4 * n + 4, :]).then_inc(x_loaded[n], 16)
                load(first, 0, n, first=True)
            sp.dma_start(taps[:, :, :], conv_in).then_inc(const_loaded, 16)
            sp.dma_start(freq[:, :], freq_in).then_inc(const_loaded, 16)
            sp.dma_start(pos_i[:, :], pos_in).then_inc(const_loaded, 16)
            for phase in phases:
                if phase is first:
                    with sp.Fori(1, phase.n) as g:
                        for j in range(SLOTS):
                            load(phase, g, j)
                else:
                    with sp.Fori(0, phase.n) as g:
                        for j in range(SLOTS):
                            load(phase, g, j)
            for n in range(4):
                sp.wait_ge(out_ready, 4 * (n + 1))
                sp.dma_start(out[:, 4 * n:4 * n + 4, :], x[:, 4 * n:4 * n + 4, :]).then_inc(stored, 16)
            sp.wait_ge(stored, 64)

        @block.gpsimd
        def _(pool):
            pool.memset(sum_sq[:, :], 0.0).then_inc(sum_cleared, 1)
            pool.wait_ge(sum_cleared, 1)
            for n in range(4):
                pool.wait_ge(x_loaded[n], 16)
            with pool.Fori(0, KT) as m:
                pool.tensor_tensor(conv_acc[:, :], x[:, m, :], x[:, m, :], ALU.mult).then_inc(x0_sq, 1)
                pool.wait_ge(x0_sq, m + 1)
                pool.tensor_tensor(sum_sq[:, :], sum_sq[:, :], conv_acc[:, :], ALU.add).then_inc(x0_summed, 1)
                pool.wait_ge(x0_summed, m + 1)

        @block.scalar
        def _(act):
            def round_unit(phase, g, j, first=False):
                n = phase.sizes[j] * P
                act.wait_ge(raw_loaded[j], 16 * (phase.g0 + g) + 16)
                if not first:
                    act.wait_ge(unit_used, SLOTS * (phase.g0 + g) + (j + 1 - SLOTS))
                act.activation(w_hi[:, j, 0:n], raw[:, j, 0:n], ACT.Copy).then_inc(hi_ready, 1)

            stats = [0]

            def root():
                stats[0] += 1
                act.wait_ge(var_ready, stats[0])
                n = stats[0]
                dst, src = (small[:, 2:4], small[:, 0:2]) if n == KV_COL_STAT else (tb[:, :], ta[:, :])
                act.activation(dst, src, ACT.Sqrt).then_inc(root_ready, 1)

            def rounds(phase, following, work, step=1, start=0, end=None):
                def body(g, r, i):
                    round_unit(phase, g + 1, 0)
                    round_unit(phase, g + 1, 1)
                    round_unit(phase, g + 1, 2)
                    work(g, 0)
                    round_unit(phase, g + 1, 3)
                    work(g, 1)

                last = phase.n - 1
                over(act, start, last if end is None else end, body, step)
                if end is not None:
                    return
                for j in range(SLOTS):
                    if following:
                        round_unit(following, 0, j)
                    if j >= 2:
                        work(last, j - 2)

            def up_work(phase):
                def work(g, part):
                    if part == 0:
                        act.wait_ge(tile_read, g * 2 + (phase.t0 + 1))
                        act.activation(tb[:, :], ta[:, :], ACT.Silu).then_inc(gate_active, 1)
                return work

            def none(g, part):
                pass

            def conv_in_work(g, part):
                if part == 0:
                    act.wait_ge(tile_read, g * 2 + (ph["conv_in"].t0 + 1))
                    act.activation(tb[:, :], ta[:, :], ACT.Sigmoid).then_inc(glu_open, 1)

            def heads_work(g, part):
                if part == 0:
                    return
                t0 = g * 8 + ph["heads"].t0
                for tt in range(2):
                    if tt == 0:
                        act.wait_ge(tile_ready, g * 5 + 5)
                    else:
                        act.wait_ge(unit_used, SLOTS * (ph["heads"].g0 + g) + 4)
                    act.activation(value[:, tt, :], bank[2 + tt][:, 0:T], ACT.Copy,
                                   scale=rstd_kv_col[:, tt:tt + 1]).then_inc(value_ready, 1)
                for j in range(2):
                    act.wait_ge(max_ready, g * 2 + (j + 1))
                    for q in range(2):
                        act.activation(probs[:, j, q * T:(q + 1) * T], scores[j][:, q * T:(q + 1) * T], ACT.Exp,
                                       bias=row_max[:, j, q:q + 1], scale=SOFTMAX_SCALE,
                                       accum_out=row_sum[:, j, q:q + 1]).then_inc(exp_ready, 1)
                for j in range(2):
                    act.wait_ge(inv_ready, g * 2 + (j + 1))
                    for q in range(2):
                        cols = slice(q * T, (q + 1) * T)
                        act.activation(probs[:, j, cols], probs[:, j, cols], ACT.Copy,
                                       scale=row_inv[:, j, q:q + 1]).then_inc(probs_ready, 1)
                for j in range(2):
                    act.wait_ge(turned_ready, g * 2 + (j + 1))
                    act.activation(probs_t[:, j, :], turned[:, :], ACT.Copy).then_inc(probs_t_ready, 1)
                for j in range(2):
                    act.wait_ge(value_summed, g * 2 + (j + 1))
                    act.activation(attn[:, g * 2 + j, 0:T], scores[j][:, 0:T], ACT.Copy).then_inc(head_hi, 1)

            def mla_out_work(g, part):
                if part == 0:
                    act.wait_ge(tile_read, g * 2 + (ph["mla_out"].t0 + 1))
                    act.activation(tb[:, :], ta[:, :], ACT.Sigmoid).then_inc(mla_open, 1)

            def conv_gate_work(g, part):
                act.wait_ge(tile_read, g * 2 + (ph["conv_gate"].t0 + part + 1))
                act.activation(merged32[:, g * 2 + part, T:2 * T], ta[:, :], ACT.Sigmoid).then_inc(conv_open, 1)

            def centre_work(g, part):
                conv_gate_work(g, part)
                for n in range(4):
                    m = g * 8 + (4 * part + n - 8 * MEAN_AT)
                    act.wait_ge(centred, m + 1)
                    act.activation(squares[:, m, :], conv[:, m, :], ACT.Square).then_inc(centred_sq, 1)

            def ln_work(g, part):
                conv_gate_work(g, part)
                for n in range(2):
                    m = g * 4 + (2 * part + n - 4 * VAR_AT)
                    act.wait_ge(ln_scaled, m + 1)
                    act.activation(td[:, :], tc[:, :], ACT.Sigmoid, scale=gain["ln_g"][:, m, :],
                                   bias=gain["ln_b"][:, m, :]).then_inc(ln_active, 1)
                    act.activation(te[:, :], tc[:, :], ACT.Identity, scale=gain["ln_g"][:, m, :],
                                   bias=gain["ln_b"][:, m, :]).then_inc(ln_active, 1)

            act.wait_ge(const_loaded, 2 * 16)
            for m in range(KT):
                if m % 4 == 0:
                    act.wait_ge(x_loaded[m // 4], 16)
                act.activation(x0g[:, m, :], x[:, m, :], ACT.Copy, scale=gain["ffn1"][:, m, :]).then_inc(x0_scaled, 1)
                if m % 4 == 3:
                    round_unit(phases[0], 0, m // 4, first=True)
            root()
            rounds(ph["ffn1_up"], ph["ffn1_down"], up_work(ph["ffn1_up"]))
            rounds(ph["ffn1_down"], ph["conv_in"], none)
            root()
            act.wait_ge(angle_ready, 1)
            act.activation(sin[:, :], sin[:, :], ACT.Sin).then_inc(trig_ready, 1)
            act.activation(cos[:, :], cos[:, :], ACT.Sin).then_inc(trig_ready, 1)
            rounds(ph["conv_in"], ph["latents"], conv_in_work)
            latents = ph["latents"]
            for g in range(latents.n):
                for j in range(SLOTS):
                    if g + 1 < latents.n:
                        round_unit(latents, g + 1, j)
                    else:
                        round_unit(ph["heads"], 0, j)
                if g == 2:
                    root()
                    root()
            root()
            rounds(ph["heads"], ph["mla_out"], heads_work)
            rounds(ph["mla_out"], ph["conv_gate"], mla_out_work)
            rounds(ph["conv_gate"], None, conv_gate_work, 1, 0, MEAN_AT)
            rounds(ph["conv_gate"], None, centre_work, 1, MEAN_AT, VAR_AT)
            root()
            rounds(ph["conv_gate"], ph["conv_out"], ln_work, 1, VAR_AT)
            rounds(ph["conv_out"], ph["w_out"], none)
            rounds(ph["w_out"], ph["ffn2_up"], none)
            root()
            rounds(ph["ffn2_up"], ph["ffn2_down"], up_work(ph["ffn2_up"]))
            rounds(ph["ffn2_down"], None, none)
            root()

        @block.tensor
        def _(pe):
            def multiply(j, at, dst, moving, start, stop):
                rows = slice(at * P, (at + 1) * P)
                pe.matmul(dst[:, 0:T], w_hi[:, j, rows], moving[:, 0:T], start=start, stop=False)
                pe.matmul(dst[:, 0:T], w_hi[:, j, rows], moving[:, T:2 * T], start=False, stop=False)
                return pe.matmul(dst[:, 0:T], w_lo[:, j, rows], moving[:, 0:T], start=False, stop=stop)

            def wait_unit(phase, g, j):
                pe.wait_ge(lo_ready, SLOTS * (phase.g0 + g) + (j + 1))

            def wait_bank(tile, in_flight=2):
                pe.wait_ge(tile_read, tile + (1 - in_flight))

            def two_tiles(phase, moving_a, moving_b=None):
                moving_b = moving_a if moving_b is None else moving_b

                def body(g, r, i, first=False):
                    for n, moving in enumerate((moving_a, moving_b)):
                        if not first:
                            wait_bank(g * 2 + (phase.t0 + n))
                        for half in range(2):
                            j = 2 * n + half
                            wait_unit(phase, g, j)
                            for i in range(8):
                                k = 8 * half + i
                                last = multiply(j, i, bank[n], moving[:, k, :], k == 0, k == KT - 1)
                            last.then_inc(unit_used, 1)
                return body

            def down(phase, moving):
                def body(g, r, i):
                    wait_bank(g + phase.t0)
                    for j in range(SLOTS):
                        wait_unit(phase, g, j)
                        for i in range(UNIT_MAX):
                            k = UNIT_MAX * j + i
                            last = multiply(j, i, bank[r], moving[:, k, :], k == 0, k == FT - 1)
                        last.then_inc(unit_used, 1)
                return body

            def total(src):
                pe.matmul(misc[:, 0:T], ones, src, start=True, stop=True).then_inc(total_ready, 1)

            pe.wait_ge(const_loaded, 2 * 16)
            pe.wait_ge(x0_split, 4)
            phase = ph["ffn1_up"]
            two_tiles(phase, h)(0, 0, 0, first=True)
            pe.wait_ge(x0_summed, KT)
            total(sum_sq[:, :])
            with pe.Fori(1, phase.n) as g:
                two_tiles(phase, h)(g, 0, 0)

            pe.wait_ge(hidden_split, FT)
            over(pe, 0, KT, down(ph["ffn1_down"], hidden), 2)
            pe.wait_ge(summed, KT)
            total(sum_sq[:, :])
            pe.wait_ge(pos_float, 1)
            pe.wait_ge(var_ready, 2)
            pe.matmul(misc[:, T:2 * T], ones[0:1, :], pos_f, start=True, stop=True).then_inc(pos_spread, 1)

            pe.wait_ge(absorbed, KT)
            over(pe, 0, KT, two_tiles(ph["conv_in"], h))

            latents = ph["latents"]
            for g in range(latents.n):
                two_tiles(latents, h)(g, 0, 0)
                if g == 2:
                    pe.wait_ge(summed, KT + KVT)
                    total(sum_sq[:, :])
                    for tt in range(2):
                        last = pe.matmul(misc[:, T + tt:T + tt + 1], sum_sq[:, tt * P:(tt + 1) * P], ones[:, 0:1],
                                         start=True, stop=True)
                    last.then_inc(total_ready, 1)
            pe.wait_ge(summed, KT + KVT + QT)
            total(sum_sq[:, :])
            pe.wait_ge(absorbed, KT + KVT + QT)

            heads = ph["heads"]

            def head_pair(g, r, i):
                t0 = g * 6 + heads.t0
                wait_unit(heads, g, 0)
                for k in range(QT):
                    last = multiply(0, k, bank[0], c_q[:, k, :], k == 0, k == QT - 1)
                last.then_inc(tile_ready, 1)
                for k in range(3):
                    last = multiply(0, QT + k, bank[1], c_q[:, k, :], k == 0, False)
                last.then_inc(unit_used, 1)
                wait_unit(heads, g, 1)
                for k in range(3):
                    last = multiply(1, k, bank[1], c_q[:, 3 + k, :], False, k == 2)
                last.then_inc(tile_ready, 1)
                for k in range(QT):
                    last = multiply(1, 3 + k, bank[2], c_q[:, k, :], k == 0, k == QT - 1)
                last.then_inc(unit_used, 1)
                wait_unit(heads, g, 2)
                for j in range(2):
                    if j == 1:
                        pe.wait_ge(tile_read, t0 + 1)
                    for k in range(KVT):
                        last = multiply(2, KVT * j + k, bank[3 - 3 * j], c_kv[:, k, :], k == 0, k == KVT - 1)
                    last.then_inc((tile_ready, unit_used)[j], 1)
                pe.wait_ge(tile_read, t0 + 2)
                pe.matmul(bank[1][:, 0:T], swap, rope_raw[:, :], start=True, stop=True).then_inc(tile_ready, 1)
                wait_unit(heads, g, 3)
                for tt in range(2):
                    pe.wait_ge(tile_read, t0 + (3 + tt))
                    dst = bank[2 + tt][:, 0:T]
                    for k in range(KVT):
                        hi = w_hi[:, 3, 2 * k * P:2 * (k + 1) * P]
                        lo = w_lo[:, 3, 2 * k * P:2 * (k + 1) * P]
                        c_hi = c_kv[:, k, tt * P:(tt + 1) * P]
                        c_lo = c_kv[:, k, T + tt * P:T + (tt + 1) * P]
                        pe.matmul(dst, c_hi, hi, start=(k == 0), stop=False)
                        pe.matmul(dst, c_lo, hi, start=False, stop=False)
                        last = pe.matmul(dst, c_hi, lo, start=False, stop=(k == KVT - 1))
                    last.then_inc((tile_ready, unit_used)[tt], 1)
                pe.wait_ge(head_step, g * 2 + 2)
                pe.wait_ge(value_ready, g * 2 + 2)
                for j in range(2):
                    rows = slice(ROPE * j, ROPE * (j + 1))
                    for q in range(2):
                        cols = slice(q * P, (q + 1) * P)
                        dst = scores[j][:, q * T:(q + 1) * T]
                        pe.matmul(dst, q_nope[:, j, cols], k_nope[:, j, :], start=True, stop=False)
                        last = pe.matmul(dst, q_rope[rows, cols], k_rope[rows, :], start=False, stop=True)
                    last.then_inc(scores_ready, 1)
                for j in range(2):
                    pe.wait_ge(probs_ready, g * 4 + (2 * j + 2))
                    for q in range(2):
                        for k in range(2):
                            last = pe.transpose(turned[:, k * T + q * P:k * T + (q + 1) * P],
                                                probs[:, j, q * T + k * P:q * T + (k + 1) * P], identity)
                    last.then_inc(turned_ready, 1)
                    pe.wait_ge(probs_t_ready, g * 2 + (j + 1))
                    for k in range(2):
                        last = pe.matmul(scores[j][:, 0:T], value[:, k, j * P:(j + 1) * P],
                                         probs_t[:, j, k * T:(k + 1) * T], start=(k == 0), stop=(k == 1))
                    last.then_inc(value_summed, 1)

            over(pe, 0, heads.n, head_pair)
            pe.wait_ge(head_split, N_HEADS)
            over(pe, 0, KT, two_tiles(ph["mla_out"], h, attn))
            gates = two_tiles(ph["conv_gate"], h)
            over(pe, 0, MEAN_AT, gates)
            pe.wait_ge(tap_done, KT * TAPS)
            for m in range(KT):
                last = pe.matmul(misc[:, 0:T], ones, conv[:, m, :], start=(m == 0), stop=(m == KT - 1))
            last.then_inc(total_ready, 1)
            over(pe, MEAN_AT, VAR_AT, gates)
            for m in range(KT):
                pe.wait_ge(centred_sq, m + 1)
                last = pe.matmul(misc[:, T:2 * T], ones, squares[:, m, :], start=(m == 0), stop=(m == KT - 1))
            last.then_inc(total_ready, 1)
            over(pe, VAR_AT, KT // 2, gates)
            pe.wait_ge(ln_split, KT)
            over(pe, 0, KT // 2, two_tiles(ph["conv_out"], attn))
            pe.wait_ge(merge_split, KT)
            over(pe, 0, KT // 2, two_tiles(ph["w_out"], merged))
            n = 2 * KT + KVT + QT
            pe.wait_ge(summed, n)
            total(sum_sq[:, :])
            pe.wait_ge(absorbed, n)
            over(pe, 0, FT, two_tiles(ph["ffn2_up"], h))
            pe.wait_ge(hidden_split, 2 * FT)
            over(pe, 0, KT, down(ph["ffn2_down"], hidden), 2)
            pe.wait_ge(summed, n + KT)
            total(sum_sq[:, :])

        @block.vector
        def _(dve):
            def split_unit(phase, g, j):
                n = phase.sizes[j] * P
                dve.wait_ge(hi_ready, SLOTS * (phase.g0 + g) + (j + 1))
                dve.tensor_tensor(w_lo[:, j, 0:n], raw[:, j, 0:n], w_hi[:, j, 0:n], ALU.subtract).then_inc(lo_ready, 1)

            def rounds(phase, following, work, step=1, start=0, end=None, between=None):
                def body(g, r, i, next_phase=phase, next_g=None):
                    next_g = g + 1 if next_g is None else next_g

                    def split(j):
                        if next_phase:
                            split_unit(next_phase, next_g, j)

                    split(0)
                    split(1)
                    work(g, 0, r, i)
                    split(2)
                    if between:
                        between(g)
                    split(3)
                    work(g, 1, r, i)

                last = phase.n - 1
                over(dve, start, last if end is None else end, body, step)
                if end is None:
                    body(last, (last - start) % step, (last - start) // step, following, 0)

            def times(dst, src, factor, tile, complete):
                dve.wait_ge(*complete)
                dve.tensor_tensor(dst, src[:, 0:T], factor, ALU.mult).then_inc(tile_read, 1)
                dve.wait_ge(tile_read, tile + 1)

            def after_unit(phase, g, j):
                return unit_used, SLOTS * (phase.g0 + g) + (j + 1)

            def absorb(n, src, g_col, dst, ready=None):
                dve.tensor_tensor(sq[:, :], src, src, ALU.mult).then_inc(squared, 1)
                if g_col is not None:
                    dve.tensor_scalar(scaled[:, :], src, g_col, None, ALU.mult).then_inc(gained, 1)
                dve.wait_ge(squared, n + 1)
                dve.tensor_tensor(sum_sq[:, :], sum_sq[:, :], sq[:, :], ALU.add).then_inc(summed, 1)
                if g_col is not None:
                    dve.wait_ge(gained, n + 1)
                    dve.tensor_scalar(dst[:, 0:T], scaled[:, :], 1.0, None, ALU.mult).then_inc(rounded, 1)
                    dve.wait_ge(rounded, n + 1)
                    dve.tensor_tensor(dst[:, T:2 * T], scaled[:, :], dst[:, 0:T], ALU.subtract).then_inc(absorbed, 1)
                dve.wait_ge(summed, n + 1)

            stats, clears, st = [0], [0], [0]

            def linked(ins):
                st[0] += 1
                ins.then_inc(stat_step, 1)
                dve.wait_ge(stat_step, st[0])

            def clear_sum():
                clears[0] += 1
                dve.memset(sum_sq[:, :], 0.0).then_inc(sums_cleared, 1)
                dve.wait_ge(sums_cleared, clears[0])

            def inverse_root(dst, dim, src=None):
                stats[0] += 1
                n = stats[0]
                src = misc[:, 0:T] if src is None else src
                var, root = (small[:, 0:2], small[:, 2:4]) if n == KV_COL_STAT else (ta[:, :], tb[:, :])
                dve.wait_ge(total_ready, TOTAL_OF_STAT[n])
                dve.tensor_scalar(var, src, 1.0 / dim, EPS, ALU.mult, ALU.add).then_inc(var_ready, 1)
                dve.wait_ge(var_ready, n)
                dve.wait_ge(root_ready, n)
                linked(dve.reciprocal(dst, root))
                linked(dve.tensor_tensor(root, dst, dst, ALU.mult))
                linked(dve.tensor_tensor(root, root, var, ALU.mult))
                linked(dve.tensor_scalar(root, root, -0.5, 1.5, ALU.mult, ALU.add))
                linked(dve.tensor_tensor(dst, dst, root, ALU.mult))

            for n in range(4):
                tiles = slice(4 * n, 4 * n + 4)
                dve.wait_ge(x0_scaled, 4 * n + 4)
                dve.tensor_copy(h[:, tiles, 0:T], x0g[:, tiles, :]).then_inc(x0_rounded, 1)
                dve.wait_ge(x0_rounded, n + 1)
                dve.tensor_tensor(h[:, tiles, T:2 * T], x0g[:, tiles, :], h[:, tiles, 0:T],
                                  ALU.subtract).then_inc(x0_split, 1)
                split_unit(phases[0], 0, n)
            inverse_root(rstd[:, :], D)

            def up_work(phase, before):
                def work(g, part, r, i):
                    if part == 0:
                        times(ta[:, :], bank[0], rstd[:, :], g * 2 + phase.t0, after_unit(phase, g, 1))
                        return
                    times(tc[:, :], bank[1], rstd[:, :], g * 2 + (phase.t0 + 1), after_unit(phase, g, 3))
                    dve.wait_ge(gate_active, g + (before + 1))
                    dve.tensor_tensor(tc[:, :], tc[:, :], tb[:, :], ALU.mult).then_inc(hidden_ready, 1)
                    dve.wait_ge(hidden_ready, g + (before + 1))
                    dve.tensor_scalar(hidden[:, g, 0:T], tc[:, :], 1.0, None, ALU.mult).then_inc(hidden_hi, 1)
                    dve.wait_ge(hidden_hi, g + (before + 1))
                    dve.tensor_tensor(hidden[:, g, T:2 * T], tc[:, :], hidden[:, g, 0:T],
                                      ALU.subtract).then_inc(hidden_split, 1)
                return work

            def residual_work(phase, factor, name, absorbed_before, tiles=1):
                def work(g, part, r, i):
                    if tiles == 1 and part == 0:
                        return
                    m = g if tiles == 1 else g * 2 + part
                    b = bank[r if tiles == 1 else part]
                    dve.wait_ge(*after_unit(phase, g, 3 if tiles == 1 else 2 * part + 1))
                    dve.scalar_tensor_tensor(out=x[:, m, :], in0=b[:, 0:T], scalar=factor, in1=x[:, m, :],
                                             op0=ALU.mult, op1=ALU.add).then_inc(tile_read, 1)
                    dve.wait_ge(tile_read, m + (phase.t0 + 1))
                    g_col = None if name is None else gain[name][:, m, :]
                    absorb(m + absorbed_before, x[:, m, :], g_col, h[:, m, :])
                return work

            rounds(ph["ffn1_up"], ph["ffn1_down"], up_work(ph["ffn1_up"], 0))
            clear_sum()
            rounds(ph["ffn1_down"], ph["conv_in"], residual_work(ph["ffn1_down"], 0.5, "mix", 0), 2)
            dve.memset(padded[:, :, 0:PAD], 0.0).then_inc(pads_cleared, 1)
            dve.memset(padded[:, :, PAD + T:T + 2 * PAD], 0.0).then_inc(pads_cleared, 1)
            dve.wait_ge(pads_cleared, 2)
            dve.wait_ge(const_loaded, 5 * 16)
            dve.tensor_copy(pos_f, pos_i[:, :]).then_inc(pos_float, 1)
            inverse_root(rstd[:, :], D)
            dve.wait_ge(pos_spread, 1)
            linked(dve.tensor_scalar(rope_raw[:, :], misc[:, T:2 * T], freq[:, 0:1], None, ALU.mult))
            for table, shift in ((sin, 0.0), (cos, 0.25)):
                linked(dve.tensor_scalar(tc[:, :], rope_raw[:, :], 1.0 / (2.0 * np.pi), shift, ALU.mult, ALU.add))
                linked(dve.tensor_scalar(tc[:, :], tc[:, :], ROUNDER, ROUNDER, ALU.add, ALU.subtract))
                src = rope_raw
                for c in TWO_PI_PARTS:
                    linked(dve.scalar_tensor_tensor(out=table[:, :], in0=tc[:, :], scalar=-c, in1=src[:, :],
                                                    op0=ALU.mult, op1=ALU.add))
                    src = table
                linked(dve.tensor_scalar(table[:, :], table[:, :], shift * 2.0 * np.pi, None, ALU.add))
                linked(dve.tensor_scalar(table[:, :], table[:, :], -PI_BELOW, PI_BELOW, ALU.max, ALU.min))
            dve.tensor_scalar(table[:, 0:1], table[:, 0:1], 0.0, None, ALU.add).then_inc(angle_ready, 1)
            dve.wait_ge(angle_ready, 1)
            dve.wait_ge(trig_ready, 2)
            linked(dve.tensor_scalar(sin[:, :], sin[:, :], freq[:, 1:2], None, ALU.mult))

            def convolve(m, part, parts):
                for n in range(part * TAPS // parts, (part + 1) * TAPS // parts):
                    t = TAP_ORDER[n]
                    src, weight = padded[:, m, t:t + T], taps[:, m, t:t + 1]
                    if n == 0:
                        dve.tensor_scalar(conv_acc[:, :], src, weight, taps[:, m, TAPS:TAPS + 1],
                                          ALU.mult, ALU.add).then_inc(tap_done, 1)
                    else:
                        dve.wait_ge(tap_done, m * TAPS + n)
                        dst = conv[:, m, :] if n == TAPS - 1 else conv_acc[:, :]
                        dve.scalar_tensor_tensor(out=dst, in0=src, scalar=weight, in1=conv_acc[:, :],
                                                 op0=ALU.mult, op1=ALU.add).then_inc(tap_done, 1)

            def conv_in_work(g, part, r, i):
                phase = ph["conv_in"]
                if part == 0:
                    times(ta[:, :], bank[0], rstd[:, :], g * 2 + phase.t0, after_unit(phase, g, 1))
                    return
                times(tc[:, :], bank[1], rstd[:, :], g * 2 + (phase.t0 + 1), after_unit(phase, g, 3))
                dve.wait_ge(glu_open, g + 1)
                dve.tensor_tensor(conv[:, g, :], tc[:, :], tb[:, :], ALU.mult).then_inc(glu_ready, 1)
                if not (isinstance(g, int) and g == KT - 1):
                    dve.wait_ge(glu_ready, g + 1)
                    convolve(i, r, 3)

            rounds(ph["conv_in"], ph["latents"], conv_in_work, 3)

            latents = ph["latents"]
            clear_sum()

            def latent(tile, n, g_col, dst):
                times(tc[:, :], bank[tile % 2], rstd[:, :], latents.t0 + tile,
                      after_unit(latents, tile // 2, 2 * (tile % 2) + 1))
                absorb(KT + n, tc[:, :], g_col, dst)

            for g in range(latents.n):
                for part in range(2):
                    if g + 1 < latents.n:
                        split_unit(latents, g + 1, 2 * part)
                        split_unit(latents, g + 1, 2 * part + 1)
                    else:
                        split_unit(ph["heads"], 0, 2 * part)
                        split_unit(ph["heads"], 0, 2 * part + 1)
                    tile = 2 * g + part
                    if g < 2:
                        latent(tile, tile, gain["kv"][:, tile, :], c_kv[:, tile, :])
                    elif g == 2:
                        dst = td if part else tc
                        times(dst[:, :], bank[part], rstd[:, :], latents.t0 + tile, after_unit(latents, g, 2 * part + 1))
                        linked(dve.tensor_tensor(dst[:, :], dst[:, :], (sin if part else cos)[:, :], ALU.mult))
                        if part:
                            linked(dve.tensor_tensor(k_rope[:, :], tc[:, :], td[:, :], ALU.add))
                            inverse_root(rstd_kv[:, :], KV_RANK)
                            inverse_root(rstd_kv_col[:, :], KV_RANK, misc[:, T:T + 2])
                            clear_sum()
                    else:
                        n = tile - 6
                        latent(tile, KVT + n, gain["q"][:, n, :], c_q[:, n, :])
                convolve(KT // 3 + g // 3, g % 3, 3)
            inverse_root(rstd_q[:, :], Q_RANK)

            heads = ph["heads"]

            def keys_work(g):
                t0 = g * 6 + heads.t0
                times(k_nope[:, 0, :], bank[3], rstd_kv[:, :], t0 + 3, (tile_ready, g * 5 + 3))
                times(k_nope[:, 1, :], bank[0], rstd_kv[:, :], t0 + 4, after_unit(heads, g, 2))

            def heads_work(g, part, r, i):
                t0 = g * 6 + heads.t0
                if part == 0:
                    times(q_nope[:, 0, :], bank[0], rstd_q[:, :], t0, (tile_ready, g * 5 + 1))
                    times(rope_raw[:, :], bank[1], rstd_q[:, :], t0 + 1, (tile_ready, g * 5 + 2))
                    times(q_nope[:, 1, :], bank[2], rstd_q[:, :], t0 + 2, after_unit(heads, g, 1))
                    return
                dve.tensor_tensor(tc[:, :], rope_raw[:, :], cos[:, :], ALU.mult).then_inc(head_step, 1)
                dve.wait_ge(tile_ready, g * 5 + 4)
                dve.tensor_tensor(td[:, :], bank[1][:, 0:T], sin[:, :], ALU.mult).then_inc(tile_read, 1)
                dve.wait_ge(tile_read, t0 + 6)
                dve.wait_ge(head_step, g * 2 + 1)
                dve.tensor_tensor(q_rope[:, :], tc[:, :], td[:, :], ALU.add).then_inc(head_step, 1)
                dve.wait_ge(head_step, g * 2 + 2)
                for j in range(2):
                    dve.wait_ge(scores_ready, g * 2 + (j + 1))
                    dve.tensor_reduce(row_inv[:, j, :], scores[j][:, :].rearrange("p (q k) -> p q k", q=2), AX.X,
                                      ALU.max).then_inc(max_step, 1)
                    dve.wait_ge(max_step, g * 2 + (j + 1))
                    dve.tensor_scalar(row_max[:, j, :], row_inv[:, j, :], -SOFTMAX_SCALE, None,
                                      ALU.mult).then_inc(max_ready, 1)
                for j in range(2):
                    dve.wait_ge(exp_ready, g * 4 + (2 * j + 2))
                    dve.reciprocal(row_inv[:, j, :], row_sum[:, j, :]).then_inc(inv_ready, 1)
                convolve(i + HEADS_TILE, r, 2)
                for j in range(2):
                    dve.wait_ge(head_hi, g * 2 + (j + 1))
                    dve.tensor_tensor(attn[:, g * 2 + j, T:2 * T], scores[j][:, 0:T],
                                      attn[:, g * 2 + j, 0:T], ALU.subtract).then_inc(head_split, 1)

            rounds(heads, ph["mla_out"], heads_work, 2, between=keys_work)

            def mla_out_work(g, part, r, i):
                phase = ph["mla_out"]
                if part == 0:
                    times(ta[:, :], bank[0], rstd[:, :], g * 2 + phase.t0, after_unit(phase, g, 1))
                    return
                dve.wait_ge(mla_open, g + 1)
                times(merged32[:, g, 0:T], bank[1], tb[:, :], g * 2 + (phase.t0 + 1), after_unit(phase, g, 3))
                if not (isinstance(g, int) and g == KT - 1):
                    convolve(i + (HEADS_TILE + heads.n // 2), r, 3)

            rounds(ph["mla_out"], ph["conv_gate"], mla_out_work, 3)

            def conv_gate_work(g, part, r, i):
                phase = ph["conv_gate"]
                m = g * 2 + part
                if not (isinstance(g, int) and g == 0 and part == 0):
                    dve.wait_ge(conv_open, m)
                times(ta[:, :], bank[part], rstd[:, :], m + phase.t0, after_unit(phase, g, 2 * part + 1))

            def centre_work(g, part, r, i):
                conv_gate_work(g, part, r, i)
                for n in range(4):
                    m = g * 8 + (4 * part + n - 8 * MEAN_AT)
                    dve.tensor_tensor(conv[:, m, :], conv[:, m, :], mean[:, :], ALU.subtract).then_inc(centred, 1)

            def ln_work(g, part, r, i):
                conv_gate_work(g, part, r, i)
                for n in range(2):
                    m = g * 4 + (2 * part + n - 4 * VAR_AT)
                    dve.tensor_tensor(tc[:, :], conv[:, m, :], rstd_ln[:, :], ALU.mult).then_inc(ln_scaled, 1)
                    dve.wait_ge(ln_active, m * 2 + 2)
                    dve.tensor_tensor(tb[:, :], te[:, :], td[:, :], ALU.mult).then_inc(ln_ready, 1)
                    dve.wait_ge(ln_ready, m + 1)
                    dve.tensor_scalar(attn[:, m, 0:T], tb[:, :], 1.0, None, ALU.mult).then_inc(ln_hi, 1)
                    dve.wait_ge(ln_hi, m + 1)
                    dve.tensor_tensor(attn[:, m, T:2 * T], tb[:, :], attn[:, m, 0:T], ALU.subtract).then_inc(ln_split, 1)

            rounds(ph["conv_gate"], None, conv_gate_work, 1, 0, MEAN_AT)
            dve.wait_ge(total_ready, TOTAL_OF_MEAN)
            dve.tensor_scalar(mean[:, :], misc[:, 0:T], 1.0 / D, None, ALU.mult).then_inc(mean_ready, 1)
            dve.wait_ge(mean_ready, 1)
            rounds(ph["conv_gate"], None, centre_work, 1, MEAN_AT, VAR_AT)
            inverse_root(rstd_ln[:, :], D, misc[:, T:2 * T])
            rounds(ph["conv_gate"], ph["conv_out"], ln_work, 1, VAR_AT)
            dve.wait_ge(conv_open, KT)

            def conv_out_work(g, part, r, i):
                phase = ph["conv_out"]
                m = g * 2 + part
                times(tb[:, :], bank[part], merged32[:, m, T:2 * T], m + phase.t0,
                      after_unit(phase, g, 2 * part + 1))
                dve.tensor_tensor(tc[:, :], tb[:, :], merged32[:, m, 0:T], ALU.add).then_inc(merge_step, 1)
                dve.wait_ge(merge_step, m + 1)
                dve.tensor_scalar(merged[:, m, 0:T], tc[:, :], 1.0, None, ALU.mult).then_inc(merge_hi, 1)
                dve.wait_ge(merge_hi, m + 1)
                dve.tensor_tensor(merged[:, m, T:2 * T], tc[:, :], merged[:, m, 0:T],
                                  ALU.subtract).then_inc(merge_split, 1)

            rounds(ph["conv_out"], ph["w_out"], conv_out_work)
            clear_sum()
            n = KT + KVT + QT
            rounds(ph["w_out"], ph["ffn2_up"], residual_work(ph["w_out"], 1.0, "ffn2", n, 2))
            inverse_root(rstd[:, :], D)
            rounds(ph["ffn2_up"], ph["ffn2_down"], up_work(ph["ffn2_up"], FT))
            clear_sum()
            rounds(ph["ffn2_down"], None, residual_work(ph["ffn2_down"], 0.5, None, n + KT), 2)
            inverse_root(rstd[:, :], D)
            for m in range(KT):
                dve.scalar_tensor_tensor(out=x[:, m, :], in0=x[:, m, :], scalar=gain["final"][:, m, :],
                                         in1=rstd[:, :], op0=ALU.mult, op1=ALU.mult).then_inc(out_ready, 1)


KV_COL_STAT = 4
TOTAL_OF_STAT = {1: 1, 2: 2, 3: 4, 4: 4, 5: 5, 6: 7, 7: 8, 8: 9}
TOTAL_OF_MEAN = 6
MEAN_AT, VAR_AT = 2, 4
HEADS_TILE = 7
TAP_ORDER = [t for t in range(TAPS) if t != PAD] + [PAD]
ROUNDER = 1.5 * 2.0 ** 23
PI_BELOW = 3.1415925
TWO_PI_PARTS = (6.25, 17.0 / 512.0, -1.7821788787841797e-05, 3.968374073792802e-09)


def tiled(w):
    k, m = w.shape
    return w.reshape(k // P, P, m // P, P).transpose(2, 0, 1, 3)


def units(tiles, per_unit):
    *lead, n, rows, cols = tiles.shape
    t = tiles.reshape(*lead, n // per_unit, per_unit, rows, cols)
    t = np.swapaxes(t, -3, -2)
    return t.reshape(*lead, n // per_unit, rows, per_unit * cols)


def halves(*columns):
    pair = np.stack([units(c, KT // 2) for c in columns], 1)
    return pair.reshape(-1, P, KT // 2 * P)


def head_stream(w_uq, w_ukv):
    q = w_uq.reshape(QT, P, N_HEADS // 2, 2, HEAD_DIM)
    kv = w_ukv.reshape(KVT, P, N_HEADS // 2, 2, 2 * P)
    q_nope = q[..., :P].transpose(2, 3, 0, 1, 4)
    rope = q[..., P:].transpose(2, 0, 1, 3, 4).reshape(N_HEADS // 2, QT, P, P)
    k_nope = kv[..., :P].transpose(2, 3, 0, 1, 4)
    v = kv[..., P:].transpose(2, 0, 3, 1, 4)
    out = np.zeros((N_HEADS // 2, SLOTS, P, 9 * P), w_uq.dtype)
    join = np.concatenate
    out[:, 0] = units(join([q_nope[:, 0], rope[:, :3]], 1), 9)[:, 0]
    out[:, 1] = units(join([rope[:, 3:], q_nope[:, 1]], 1), 9)[:, 0]
    out[:, 2, :, :8 * P] = units(join([k_nope[:, 0], k_nope[:, 1]], 1), 8)[:, 0]
    out[:, 3, :, :8 * P] = units(v.reshape(N_HEADS // 2, 2 * KVT, P, P), 8)[:, 0]
    return out.reshape(-1, P, 9 * P)


def columns(v):
    return v.reshape(-1, P).T[:, :, None]


def kernel(**inputs):
    import concourse.bacc as _bacc
    from concourse.bass_utils import run_bass_kernel_spmd as _run

    a = {k: np.asarray(v) for k, v in inputs.items()}
    w = {k: v[0] for k, v in a.items() if v.ndim == 3 and k != "x"}
    v = {k: a[k][0] for k in a if a[k].ndim == 2 and k != "positions"}

    cuts = np.cumsum([0, D, D, Q_RANK, KV_RANK, ROPE, D, D])
    conv_a, conv_g, q_down, kv_down, k_rope, gate_conv, gate_mla = (
        w["w_in"][:, lo:hi] for lo, hi in zip(cuts[:-1], cuts[1:]))
    half = ROPE // 2
    swapped = np.concatenate([k_rope[:, half:], k_rope[:, :half]], 1)
    latents = np.concatenate([kv_down, k_rope, k_rope, swapped, swapped, q_down], 1)

    def up(n):
        return halves(tiled(w[f"ffn{n}_w_gate"]), tiled(w[f"ffn{n}_w_up"]))

    def down(n):
        return units(tiled(w[f"ffn{n}_w_down"]), UNIT_MAX).reshape(-1, P, UNIT_MAX * P)

    arrays = {
        "ffn1_up": up(1),
        "ffn1_down": down(1),
        "conv_in": halves(tiled(conv_g), tiled(conv_a)),
        "latents": halves(tiled(latents)),
        "heads": head_stream(w["mla_w_uq"], w["mla_w_ukv"]),
        "mla_out": halves(tiled(gate_mla), tiled(w["mla_w_o"])),
        "conv_gate": halves(tiled(gate_conv)),
        "conv_out": halves(tiled(w["conv_w_pw_out"])),
        "w_out": halves(tiled(w["w_out"])),
        "ffn2_up": up(2),
        "ffn2_down": down(2),
    }
    names = list(arrays)
    arrays["x_in"] = a["x"][0].T.reshape(KT, P, T).transpose(1, 0, 2)
    arrays["pos_in"] = a["positions"]
    arrays["gains_in"] = np.concatenate([columns(g) for g in (
        v["ffn1_norm_g"], v["mix_norm_g"], v["ffn2_norm_g"], a["final_norm_g"], v["conv_ln_g"], v["conv_ln_b"],
        v["mla_q_norm_g"], v["mla_kv_norm_g"])], 1)
    per_channel = np.concatenate([w["conv_w_dw"], a["conv_b_dw"]], 0)
    arrays["conv_in_w"] = per_channel.reshape(TAPS + 1, KT, P).transpose(2, 1, 0)
    eye = np.eye(P, dtype=np.float32)
    arrays["const_in"] = np.concatenate([eye, eye[np.arange(P) ^ half], np.ones((P, P), np.float32)], 1)
    place = np.arange(P) % ROPE
    inverse = 10000.0 ** (-2.0 * (place % half) / ROPE)
    arrays["freq_in"] = np.stack([inverse, np.where(place < half, -1.0, 1.0)], 1).astype(np.float32)

    nc = _bacc.Bacc("TRN2", target_bir_lowering=False, num_devices=1, dynamic_dma_scratch_size=1024)
    handles, feeds = {}, {}
    for name, array in arrays.items():
        array = np.ascontiguousarray(array)
        feeds[f"in_{name}"] = array
        handles[name] = nc.dram_tensor(f"in_{name}", array.shape, mybir.dt.from_np(array.dtype),
                                       kind="ExternalInput").ap()
    out = nc.dram_tensor("out", (P, KT, T), F32, kind="ExternalOutput").ap()
    encoder(nc, {n: handles[n] for n in names}, handles["x_in"], handles["pos_in"], handles["gains_in"],
            handles["conv_in_w"], handles["const_in"], handles["freq_in"], out)
    r = _run(nc, [feeds], core_ids=[0])
    got = r.results[0]["out"]
    return np.ascontiguousarray(got.transpose(2, 1, 0).reshape(1, T, D))
```

```python
from contextlib import ExitStack

import numpy as np

import concourse.bass as bass
from concourse import mybir

F32 = mybir.dt.float32
F32R = mybir.dt.float32r
I32 = mybir.dt.int32
ALU = mybir.AluOpType
ACT = mybir.ActivationFunctionType
AX = mybir.AxisListType

P = 128
T = 256
D = 2048
KT = D // P
D_FF = 5632
FT = D_FF // P
N_HEADS = 16
ROPE = 64
KV_RANK = 512
Q_RANK = 768
KVT = KV_RANK // P
QT = Q_RANK // P
TAPS = 31
PAD = TAPS // 2
HEAD_DIM = P + ROPE
SOFTMAX_SCALE = float(HEAD_DIM) ** -0.5
EPS = 1e-6
SLOTS = 4
UNIT_MAX = FT // 4

PHASES = [
    ("ffn1_up", FT, (8, 8, 8, 8), 2),
    ("ffn1_down", KT, (FT // 4,) * 4, 1),
    ("conv_in", KT, (8, 8, 8, 8), 2),
    ("latents", 6, (8, 8, 8, 8), 2),
    ("heads", N_HEADS // 2, (9, 9, 8, 8), 6),
    ("mla_out", KT, (8, 8, 8, 8), 2),
    ("conv_gate", KT // 2, (8, 8, 8, 8), 2),
    ("conv_out", KT // 2, (8, 8, 8, 8), 2),
    ("w_out", KT // 2, (8, 8, 8, 8), 2),
    ("ffn2_up", FT, (8, 8, 8, 8), 2),
    ("ffn2_down", KT, (FT // 4,) * 4, 1),
]


class Phase:

    def __init__(self, name, n, sizes, g0, t0):
        self.name, self.n, self.sizes, self.g0, self.t0 = name, n, sizes, g0, t0


def plan():
    out, group, tile = [], 0, 0
    for name, n, sizes, tiles in PHASES:
        out.append(Phase(name, n, sizes, group, tile))
        group += n
        tile += n * tiles
    return out


def encoder(nc, streams, x_in, pos_in, gains_in, conv_in, const_in, freq_in, out):
    phases = plan()
    ph = {p.name: p for p in phases}

    with ExitStack() as ctx:
        def sb(name, shape, dt=F32, stack=ctx):
            return stack.enter_context(nc.sbuf_tensor(name, shape, dt))

        def sem(name):
            return ctx.enter_context(nc.semaphore(name))

        raw = sb("raw", [P, SLOTS, UNIT_MAX * P])
        w_hi = sb("w_hi", [P, SLOTS, UNIT_MAX * P], F32R)
        w_lo = sb("w_lo", [P, SLOTS, UNIT_MAX * P], F32R)
        x = sb("x", [P, KT, T])
        h = sb("h", [P, KT, 2 * T], F32R)
        consts = sb("consts", [P, 3 * P])
        identity, swap, ones = (consts[:, n * P:(n + 1) * P] for n in range(3))
        gains = sb("gains", [P, 6 * KT + QT + KVT, 1])
        taps = sb("taps", [P, KT, TAPS + 1])
        freq = sb("freq", [P, 2])
        rstd = sb("rstd", [P, T])
        rstd_q = sb("rstd_q", [P, T])
        rstd_kv = sb("rstd_kv", [P, T])
        rstd_kv_col = sb("rstd_kv_col", [P, 2])
        sum_sq = sb("sum_sq", [P, T])
        sq = sb("sq", [P, T])
        prod = sb("prod", [P, T])
        ta = sb("ta", [P, T])
        tb = sb("tb", [P, T])
        tcd = sb("tcd", [P, 2 * T])
        tc, td = tcd[:, 0:T], tcd[:, T:2 * T]
        small = sb("small", [P, 8])
        conv_acc = sb("conv_acc", [P, 2 * T])
        pos_i = sb("pos_i", [1, T], I32)
        trig = sb("trig", [P, 2 * T])
        sin, cos = trig[:, 0:T], trig[:, T:2 * T]
        angle, turns = conv_acc, tcd
        ln_gate = (conv_acc[:, 0:T], conv_acc[:, T:2 * T], sin, cos)
        mean = rstd_kv
        rstd_ln = rstd_q
        pos_f = td[0:1, :]
        ffn = ExitStack()
        hidden = sb("hidden", [P, FT, 2 * T], F32R, ffn)
        ffn.close()
        start = ExitStack()
        sb("before_x0", [P, FT * 2 * T - KT * T], F32, start)
        x0_sq = sb("x0_sq", [P, KT, T], F32, start)
        start.close()
        padded = sb("padded", [P, KT, T + 2 * PAD])
        conv = padded[:, :, PAD:PAD + T]
        outs = ExitStack()
        squares = sb("squares", [P, KT, T], F32, outs)
        tree = sb("tree", [P, KT // 2, T], F32, outs)
        outs.close()
        attn = sb("attn", [P, KT, 2 * T], F32R)
        outs = ExitStack()
        merged32 = sb("merged32", [P, KT, 2 * T], F32, outs)
        outs.close()
        outs = ExitStack()
        merged = sb("merged", [P, KT, 2 * T], F32R, outs)
        outs.close()
        c_kv = sb("c_kv", [P, KVT, 2 * T], F32R)
        c_q = sb("c_q", [P, QT, 2 * T], F32R)
        q_nope = sb("q_nope", [P, 2, T])
        q_rope = sb("q_rope", [P, T])
        k_nope = sb("k_nope", [P, 2, T])
        value = sb("value", [P, 2, 2 * P])
        probs = sb("probs", [P, 2, 2 * T])
        probs_t = sb("probs_t", [P, 2, 2 * T])
        row_max = sb("row_max", [P, 2, 2])
        row_sum = sb("row_sum", [P, 2, 2])
        row_inv = sb("row_inv", [P, 2, 2])
        rope_raw = sb("rope_raw", [P, T])
        k_rope = sb("k_rope", [P, T])

        gain = {}
        at = 0
        for name, n in (("ffn1", KT), ("mix", KT), ("ffn2", KT), ("final", KT), ("ln_g", KT),
                        ("ln_b", KT), ("q", QT), ("kv", KVT)):
            gain[name] = gains[:, at:at + n, :]
            at += n

        bank = [ctx.enter_context(nc.psum_tensor(f"bank{n}", [P, 2 * T], F32)) for n in range(4)]
        scores = [ctx.enter_context(nc.psum_tensor(f"scores{n}", [P, 2 * T], F32)) for n in range(2)]
        turned0 = ctx.enter_context(nc.psum_tensor("turned0", [P, 2 * T], F32))
        misc = ctx.enter_context(nc.psum_tensor("misc", [P, 2 * T], F32))

        turned = (turned0, misc)

        raw_loaded = [sem(f"raw_loaded{j}") for j in range(SLOTS)]
        hi_ready = sem("hi_ready")
        lo_ready = sem("lo_ready")
        unit_used = sem("unit_used")
        tile_ready = sem("tile_ready")
        tile_read = sem("tile_read")
        x_loaded = [sem(f"x_loaded{n}") for n in range(4)]
        const_loaded = sem("const_loaded")
        gains_loaded = sem("gains_loaded")
        small_loaded = sem("small_loaded")
        x0_rounded = sem("x0_rounded")
        x0_squared = sem("x0_squared")
        x0_last_squared = sem("x0_last_squared")
        x0_split = sem("x0_split")
        x0_added = sem("x0_added")
        sums_cleared = sem("sums_cleared")
        pads_cleared = sem("pads_cleared")
        tap_done = sem("tap_done")
        squared = sem("squared")
        summed = sem("summed")
        squared_ln = sem("squared_ln")
        tree_step = sem("tree_step")
        rounded = sem("rounded")
        absorbed = sem("absorbed")
        total_ready = sem("total_ready")
        stat_step = sem("stat_step")
        var_ready = sem("var_ready")
        root_ready = sem("root_ready")
        gate_active = sem("gate_active")
        hidden_ready = sem("hidden_ready")
        hidden_hi = sem("hidden_hi")
        hidden_split = sem("hidden_split")
        glu_open = sem("glu_open")
        glu_ready = sem("glu_ready")
        pos_float = sem("pos_float")
        pos_spread = sem("pos_spread")
        angle_step = sem("angle_step")
        angle_ready = sem("angle_ready")
        trig_ready = sem("trig_ready")
        head_step = sem("head_step")
        value_ready = sem("value_ready")
        ln_scaled = sem("ln_scaled")
        scores_ready = sem("scores_ready")
        max_step = sem("max_step")
        max_ready = sem("max_ready")
        exp_ready = sem("exp_ready")
        inv_ready = sem("inv_ready")
        probs_ready = sem("probs_ready")
        turned_ready = sem("turned_ready")
        probs_t_ready = sem("probs_t_ready")
        value_summed = sem("value_summed")
        head_hi = sem("head_hi")
        head_split = sem("head_split")
        mla_open = sem("mla_open")
        mean_ready = sem("mean_ready")
        centred = sem("centred")
        conv_open = sem("conv_open")
        ln_ready = sem("ln_ready")
        ln_active = sem("ln_active")
        ln_hi = sem("ln_hi")
        ln_split = sem("ln_split")
        merge_step = sem("merge_step")
        merge_hi = sem("merge_hi")
        merge_split = sem("merge_split")
        out_ready = sem("out_ready")
        stored = sem("stored")

        block = ctx.enter_context(nc.Block())

        def over(eng, start, end, body, step=1):
            head = min(end, -(-start // step) * step)
            rolled = (end - head) // step
            rolled = rolled if rolled > 1 else 0
            for g in range(start, head):
                body(g, g % step, g // step)
            if rolled:
                with eng.Fori(head // step, head // step + rolled) as i:
                    for r in range(step):
                        body(i * step + r, r, i)
            for g in range(head + rolled * step, end):
                body(g, g % step, g // step)

        @block.sync
        def _(sp):
            sp.dma_start(gains[:, :, :], gains_in).then_inc(gains_loaded, 16)

            def load(phase, g, j, first=False):
                n = phase.sizes[j] * P
                if not first:
                    sp.wait_ge(lo_ready, SLOTS * (phase.g0 + g) + (j + 1 - SLOTS))
                sp.dma_start(raw[:, j, 0:n], streams[phase.name][g * SLOTS + j, :, 0:n]).then_inc(raw_loaded[j], 16)

            first = phases[0]
            for n in range(4):
                sp.dma_start(x[:, 4 * n:4 * n + 4, :], x_in[:, 4 * n:4 * n + 4, :]).then_inc(x_loaded[n], 16)
                load(first, 0, n, first=True)
            sp.dma_start(consts[:, :], const_in).then_inc(const_loaded, 16)
            sp.dma_start(taps[:, :, :], conv_in).then_inc(small_loaded, 16)
            sp.dma_start(freq[:, :], freq_in).then_inc(small_loaded, 16)
            sp.dma_start(pos_i[:, :], pos_in).then_inc(small_loaded, 16)
            for phase in phases:
                if phase is first:
                    with sp.Fori(1, phase.n) as g:
                        for j in range(SLOTS):
                            load(phase, g, j)
                else:
                    with sp.Fori(0, phase.n) as g:
                        for j in range(SLOTS):
                            load(phase, g, j)
            for n in range(4):
                sp.wait_ge(out_ready, 4 * (n + 1))
                sp.dma_start(out[:, 4 * n:4 * n + 4, :], x[:, 4 * n:4 * n + 4, :]).then_inc(stored, 16)
            sp.wait_ge(stored, 64)

        @block.gpsimd
        def _(pool):
            def tiles(n, first=0):
                return x0_sq[:, first:first + n, :].rearrange("p k t -> p (k t)")

            for n in range(3):
                pool.wait_ge(x_loaded[n], 16)
                src = x[:, 4 * n:4 * n + 4, :].rearrange("p k t -> p (k t)")
                pool.tensor_tensor(tiles(4, 4 * n), src, src, ALU.mult).then_inc(x0_squared, 1)
                if n:
                    pool.wait_ge(x0_squared, n + 1)
                    if n > 1:
                        pool.wait_ge(x0_added, n - 1)
                    pool.tensor_tensor(tiles(4), tiles(4), tiles(4, 4 * n), ALU.add).then_inc(x0_added, 1)
            pool.wait_ge(x0_last_squared, 1)
            pool.wait_ge(x0_added, 2)
            pool.tensor_tensor(tiles(4), tiles(4), tiles(4, 12), ALU.add).then_inc(x0_added, 1)
            pool.wait_ge(x0_added, 3)
            pool.tensor_tensor(tiles(2), tiles(2), tiles(2, 2), ALU.add).then_inc(x0_added, 1)
            pool.wait_ge(x0_added, 4)
            pool.tensor_tensor(sum_sq[:, :], tiles(1), tiles(1, 1), ALU.add).then_inc(x0_added, 1)

        @block.scalar
        def _(act):
            def round_unit(phase, g, j, first=False):
                n = phase.sizes[j] * P
                act.wait_ge(raw_loaded[j], 16 * (phase.g0 + g) + 16)
                if not first:
                    act.wait_ge(unit_used, SLOTS * (phase.g0 + g) + (j + 1 - SLOTS))
                act.activation(w_hi[:, j, 0:n], raw[:, j, 0:n], ACT.Copy).then_inc(hi_ready, 1)

            stats = [0]

            def root():
                stats[0] += 1
                act.wait_ge(var_ready, stats[0])
                n = stats[0]
                dst, src = (small[:, 2:4], small[:, 0:2]) if n == KV_COL_STAT else (tb[:, :], ta[:, :])
                act.activation(dst, src, ACT.Sqrt).then_inc(root_ready, 1)

            def rounds(phase, following, work, start=0, end=None, opening=None):
                def round_next(g, j, ahead):
                    if not isinstance(g, int) or ahead < phase.n:
                        round_unit(phase, ahead, j)
                    elif following and ahead == phase.n:
                        round_unit(following, 0, j)

                def body(g, r=0, i=0):
                    work(g, 0)
                    round_next(g, 3, g + 1)
                    work(g, 1)
                    for j in range(3):
                        round_next(g, j, g + 2)

                if start == 0:
                    for j in range(3):
                        round_next(0, j, 1)
                        if j == 0 and opening:
                            opening()
                if end is not None:
                    over(act, start, end, body)
                else:
                    over(act, start, phase.n - 2, body)
                    body(phase.n - 2)
                    body(phase.n - 1)

            def up_work(phase):
                def work(g, part):
                    if part == 0:
                        act.wait_ge(tile_read, g * 2 + (phase.t0 + 1))
                        act.activation(tb[:, :], ta[:, :], ACT.Silu).then_inc(gate_active, 1)
                return work

            def none(g, part):
                pass

            def conv_in_work(g, part):
                if part == 0:
                    act.wait_ge(tile_read, g * 2 + (ph["conv_in"].t0 + 1))
                    act.activation(tb[:, :], ta[:, :], ACT.Sigmoid).then_inc(glu_open, 1)

            def attend_exp(p):
                for j in range(2):
                    act.wait_ge(max_ready, p * 2 + (j + 1))
                    for q in range(2):
                        act.activation(probs[:, j, q * T:(q + 1) * T], scores[j][:, q * T:(q + 1) * T], ACT.Exp,
                                       bias=row_max[:, j, q:q + 1], scale=SOFTMAX_SCALE,
                                       accum_out=row_sum[:, j, q:q + 1]).then_inc(exp_ready, 1)

            def attend_scale(p):
                for j in range(2):
                    act.wait_ge(inv_ready, p * 2 + (j + 1))
                    for q in range(2):
                        cols = slice(q * T, (q + 1) * T)
                        act.activation(probs[:, j, cols], probs[:, j, cols], ACT.Copy,
                                       scale=row_inv[:, j, q:q + 1]).then_inc(probs_ready, 1)

            def attend_turn(p):
                for j in range(2):
                    act.wait_ge(turned_ready, p * 2 + (j + 1))
                    act.activation(probs_t[:, j, :], turned[j][:, :], ACT.Copy).then_inc(probs_t_ready, 1)

            def attend_out(p):
                for j in range(2):
                    act.wait_ge(value_summed, p * 2 + (j + 1))
                    act.activation(attn[:, p * 2 + j, 0:T], scores[j][:, 0:T], ACT.Copy).then_inc(head_hi, 1)

            def head_pair(g, r=0, i=0):
                heads = ph["heads"]
                first = isinstance(g, int) and g == 0
                last = isinstance(g, int) and g == heads.n - 1
                coming, n = (ph["mla_out"], 0) if last else (heads, g + 1)
                if not first:
                    attend_exp(g - 1)
                round_unit(coming, n, 0)
                if not first:
                    attend_scale(g - 1)
                round_unit(coming, n, 1)
                if not first:
                    attend_turn(g - 1)
                round_unit(coming, n, 2)
                if not first:
                    attend_out(g - 1)
                for tt in range(2):
                    if tt == 0:
                        act.wait_ge(tile_ready, g * 5 + 5)
                    else:
                        act.wait_ge(unit_used, SLOTS * (heads.g0 + g) + 4)
                    act.activation(value[:, tt, :], bank[2 + tt][:, 0:T], ACT.Copy,
                                   scale=rstd_kv_col[:, tt:tt + 1]).then_inc(value_ready, 1)
                round_unit(coming, n, 3)

            def mla_out_work(g, part):
                if part == 0:
                    act.wait_ge(tile_read, g * 2 + (ph["mla_out"].t0 + 1))
                    act.activation(tb[:, :], ta[:, :], ACT.Sigmoid).then_inc(mla_open, 1)

            def conv_gate_work(g, part):
                act.wait_ge(tile_read, g * 2 + (ph["conv_gate"].t0 + part + 1))
                act.activation(merged32[:, g * 2 + part, T:2 * T], (ta, tb)[part][:, :], ACT.Sigmoid).then_inc(conv_open, 1)

            def ln_active_tile(tile, n):
                act.wait_ge(ln_scaled, tile + (n + 1))
                channels = conv[:, tile + n, :]
                for dst, func in ((ln_gate[n], ACT.Sigmoid), (channels, ACT.Identity)):
                    act.activation(dst, channels, func, scale=gain["ln_g"][:, tile + n, :],
                                   bias=gain["ln_b"][:, tile + n, :]).then_inc(ln_active, 1)

            def gate_group(g, r=0, i=0, beside=None):
                gates = ph["conv_gate"]
                conv_gate_work(g, 0)
                last = isinstance(g, int) and g == gates.n - 1
                if last:
                    round_unit(ph["conv_out"], 0, 3)
                else:
                    round_unit(gates, g + 1, 3)
                conv_gate_work(g, 1)
                for n in range(4):
                    if beside:
                        beside(n)
                    if n < 3 and not last:
                        if isinstance(g, int) and g == gates.n - 2:
                            round_unit(ph["conv_out"], 0, n)
                        else:
                            round_unit(gates, g + 2, n)

            def square(n):
                tiles = slice(4 * n, 4 * n + 4)
                act.wait_ge(centred, 4 * n + 4)
                act.activation(squares[:, tiles, :], conv[:, tiles, :], ACT.Square).then_inc(squared_ln, 1)

            def ln_group(g, r=0, i=0):
                gate_group(g, beside=lambda n: ln_active_tile(g * 4 - 4 * LN_AT, n))

            act.wait_ge(gains_loaded, 16)
            for n in range(4):
                act.wait_ge(x_loaded[n], 16)
                for m in range(4 * n, 4 * n + 4):
                    act.activation(h[:, m, 0:T], x[:, m, :], ACT.Copy, scale=gain["ffn1"][:, m, :]).then_inc(x0_rounded, 1)
                if n == 3:
                    act.activation(x0_sq[:, 12:16, :], x[:, 12:16, :], ACT.Square).then_inc(x0_last_squared, 1)
                round_unit(phases[0], 0, n, first=True)
            rounds(ph["ffn1_up"], ph["ffn1_down"], up_work(ph["ffn1_up"]), opening=root)
            rounds(ph["ffn1_down"], ph["conv_in"], none, 0, 2)
            act.wait_ge(angle_ready, 1)
            act.activation(trig[:, :], trig[:, :], ACT.Sin).then_inc(trig_ready, 1)
            rounds(ph["ffn1_down"], ph["conv_in"], none, 2)
            rounds(ph["conv_in"], ph["latents"], conv_in_work, opening=root)
            latents = ph["latents"]
            for g in range(latents.n):
                for j in range(SLOTS):
                    if g + 1 < latents.n:
                        round_unit(latents, g + 1, j)
                    else:
                        round_unit(ph["heads"], 0, j)
                    if g != 2 and j % 2:
                        tile = 2 * g + j // 2
                        act.wait_ge(tile_read, latents.t0 + tile + 1)
                        act.activation(sq[:, :], tc[:, :], ACT.Square).then_inc(squared, 1)
                if g == 2:
                    root()
                    root()
            root()
            over(act, 0, 1, head_pair)
            over(act, 1, ph["heads"].n - 1, head_pair)
            head_pair(ph["heads"].n - 1)
            p = ph["heads"].n - 1
            attend_exp(p)
            round_unit(ph["mla_out"], 1, 0)
            attend_scale(p)
            round_unit(ph["mla_out"], 1, 1)
            attend_turn(p)
            round_unit(ph["mla_out"], 1, 2)
            mla_out_work(0, 0)
            attend_out(p)
            round_unit(ph["mla_out"], 1, 3)
            for j in range(3):
                round_unit(ph["mla_out"], 2, j)
            rounds(ph["mla_out"], ph["conv_gate"], mla_out_work, 1)
            gates = ph["conv_gate"]
            for j in range(3):
                round_unit(gates, 1, j)
            for g in range(LN_AT):
                gate_group(g, beside={CENTRE_AT: square, LN_AT - 1: lambda n: root() if n == 1 else None}.get(g))
            over(act, LN_AT, gates.n - 2, ln_group)
            ln_group(gates.n - 2)
            gate_group(gates.n - 1)
            rounds(ph["conv_out"], ph["w_out"], none)
            rounds(ph["w_out"], ph["ffn2_up"], none)
            rounds(ph["ffn2_up"], ph["ffn2_down"], up_work(ph["ffn2_up"]), opening=root)
            rounds(ph["ffn2_down"], None, none)
            root()

        @block.tensor
        def _(pe):
            def multiply(j, at, dst, moving, start, stop):
                rows = slice(at * P, (at + 1) * P)
                pe.matmul(dst[:, 0:T], w_hi[:, j, rows], moving[:, 0:T], start=start, stop=False)
                pe.matmul(dst[:, 0:T], w_hi[:, j, rows], moving[:, T:2 * T], start=False, stop=False)
                return pe.matmul(dst[:, 0:T], w_lo[:, j, rows], moving[:, 0:T], start=False, stop=stop)

            def wait_unit(phase, g, j):
                pe.wait_ge(lo_ready, SLOTS * (phase.g0 + g) + (j + 1))

            def wait_bank(tile, in_flight=2):
                pe.wait_ge(tile_read, tile + (1 - in_flight))

            def arrived(k, n, per_unit, ready, base):
                if ready is not None and (k % per_unit == 0 or k >= n - 3):
                    upto = k + 1 if k >= n - 3 else min(k + per_unit, n - 3)
                    pe.wait_ge(ready, base + upto)

            def two_tiles(phase, moving_a, moving_b=None):
                moving_b = moving_a if moving_b is None else moving_b

                def body(g, r=0, i=0, first=False, ready=None, base=0, after=(), late=0):
                    for n, moving in enumerate((moving_a, moving_b)):
                        if not first:
                            wait_bank(g * 2 + (phase.t0 + n))
                        for half in range(2):
                            j = 2 * n + half
                            wait_unit(phase, g, j)
                            for i in range(8):
                                k = 8 * half + i
                                if n == late:
                                    arrived(k, KT, 8, ready, base)
                                last = multiply(j, i, bank[n], moving[:, k, :], k == 0, k == KT - 1)
                            last.then_inc(unit_used, 1)
                            for unit, step in after:
                                if unit == j:
                                    step()
                return body

            def down(phase, moving, base):
                def body(g, r, i):
                    wait_bank(g + phase.t0)
                    for j in range(SLOTS):
                        wait_unit(phase, g, j)
                        for i in range(UNIT_MAX):
                            k = UNIT_MAX * j + i
                            if isinstance(g, int) and g == 0:
                                arrived(k, FT, UNIT_MAX, hidden_split, base)
                            last = multiply(j, i, bank[r], moving[:, k, :], k == 0, k == FT - 1)
                        last.then_inc(unit_used, 1)

                body(0, 0, 0)
                body(1, 1, 0)
                over(pe, 2, phase.n, body, 2)

            def total(src, at=0):
                pe.matmul(misc[:, at:at + T], ones, src, start=True, stop=True).then_inc(total_ready, 1)

            def positions():
                pe.wait_ge(pos_float, 1)
                pe.wait_ge(var_ready, 1)
                pe.matmul(misc[:, T:2 * T], ones[0:1, :], pos_f, start=True, stop=True).then_inc(pos_spread, 1)

            def first_total():
                pe.wait_ge(const_loaded, 16)
                pe.wait_ge(x0_added, ADDS)
                total(sum_sq[:, :])

            def total_after(sem, count, src, at=0):
                def step():
                    pe.wait_ge(sem, count)
                    total(src, at)
                return step

            phase = ph["ffn1_up"]
            two_tiles(phase, h)(0, first=True, ready=x0_split, base=0,
                                after=((1, first_total), (3, positions)))
            over(pe, 1, phase.n, two_tiles(phase, h))

            down(ph["ffn1_down"], hidden, 0)

            two_tiles(ph["conv_in"], h)(0, ready=absorbed, base=0,
                                        after=((0, total_after(summed, KT, sum_sq[:, :])),))
            over(pe, 1, KT, two_tiles(ph["conv_in"], h))

            latents = ph["latents"]
            for g in range(latents.n):
                two_tiles(latents, h)(g)
                if g == 2:
                    pe.wait_ge(summed, KT + KVT)
                    total(sum_sq[:, :])
                    for tt in range(2):
                        last = pe.matmul(misc[:, T + tt:T + tt + 1], sum_sq[:, tt * P:(tt + 1) * P], ones[:, 0:1],
                                         start=True, stop=True)
                    last.then_inc(total_ready, 1)
            pe.wait_ge(summed, KT + KVT + QT)
            total(sum_sq[:, :])
            pe.wait_ge(absorbed, KT + KVT + QT)

            heads = ph["heads"]

            def attend_scores(p):
                pe.wait_ge(head_step, p * 2 + 2)
                for j in range(2):
                    rows = slice(ROPE * j, ROPE * (j + 1))
                    for q in range(2):
                        cols = slice(q * P, (q + 1) * P)
                        dst = scores[j][:, q * T:(q + 1) * T]
                        pe.matmul(dst, q_nope[:, j, cols], k_nope[:, j, :], start=True, stop=False)
                        last = pe.matmul(dst, q_rope[rows, cols], k_rope[rows, :], start=False, stop=True)
                    last.then_inc(scores_ready, 1)

            def attend_turn(p):
                for j in range(2):
                    pe.wait_ge(probs_ready, p * 4 + (2 * j + 2))
                    for q in range(2):
                        for k in range(2):
                            last = pe.transpose(turned[j][:, k * T + q * P:k * T + (q + 1) * P],
                                                probs[:, j, q * T + k * P:q * T + (k + 1) * P], identity)
                    last.then_inc(turned_ready, 1)

            def attend_values(p):
                pe.wait_ge(value_ready, p * 2 + 2)
                for j in range(2):
                    pe.wait_ge(probs_t_ready, p * 2 + (j + 1))
                    for k in range(2):
                        last = pe.matmul(scores[j][:, 0:T], value[:, k, j * P:(j + 1) * P],
                                         probs_t[:, j, k * T:(k + 1) * T], start=(k == 0), stop=(k == 1))
                    last.then_inc(value_summed, 1)

            def head_pair(g, r=0, i=0):
                t0 = g * 6 + heads.t0
                first = isinstance(g, int) and g == 0
                if not first:
                    attend_scores(g - 1)
                wait_unit(heads, g, 0)
                for k in range(QT):
                    last = multiply(0, k, bank[0], c_q[:, k, :], k == 0, k == QT - 1)
                last.then_inc(tile_ready, 1)
                for k in range(3):
                    last = multiply(0, QT + k, bank[1], c_q[:, k, :], k == 0, False)
                last.then_inc(unit_used, 1)
                wait_unit(heads, g, 1)
                for k in range(3):
                    last = multiply(1, k, bank[1], c_q[:, 3 + k, :], False, k == 2)
                last.then_inc(tile_ready, 1)
                if not first:
                    pe.wait_ge(value_ready, g * 2)
                for k in range(QT):
                    last = multiply(1, 3 + k, bank[2], c_q[:, k, :], k == 0, k == QT - 1)
                last.then_inc(unit_used, 1)
                if not first:
                    attend_turn(g - 1)
                wait_unit(heads, g, 2)
                for j in range(2):
                    if j == 1:
                        pe.wait_ge(tile_read, t0 + 1)
                    for k in range(KVT):
                        last = multiply(2, KVT * j + k, bank[3 - 3 * j], c_kv[:, k, :], k == 0, k == KVT - 1)
                    last.then_inc((tile_ready, unit_used)[j], 1)
                pe.wait_ge(tile_read, t0 + 2)
                pe.matmul(bank[1][:, 0:T], swap, rope_raw[:, :], start=True, stop=True).then_inc(tile_ready, 1)
                if not first:
                    attend_values(g - 1)
                wait_unit(heads, g, 3)
                for tt in range(2):
                    pe.wait_ge(tile_read, t0 + (3 + tt))
                    dst = bank[2 + tt][:, 0:T]
                    for k in range(KVT):
                        hi = w_hi[:, 3, 2 * k * P:2 * (k + 1) * P]
                        lo = w_lo[:, 3, 2 * k * P:2 * (k + 1) * P]
                        c_hi = c_kv[:, k, tt * P:(tt + 1) * P]
                        c_lo = c_kv[:, k, T + tt * P:T + (tt + 1) * P]
                        pe.matmul(dst, c_hi, hi, start=(k == 0), stop=False)
                        pe.matmul(dst, c_lo, hi, start=False, stop=False)
                        last = pe.matmul(dst, c_hi, lo, start=False, stop=(k == KVT - 1))
                    last.then_inc((tile_ready, unit_used)[tt], 1)

            over(pe, 0, 1, head_pair)
            over(pe, 1, heads.n, head_pair)
            p = heads.n - 1
            attend_scores(p)
            two_tiles(ph["mla_out"], h, attn)(0, ready=head_split, base=0, late=1, after=(
                (1, lambda: attend_turn(p)), (2, lambda: attend_values(p))))
            over(pe, 1, KT, two_tiles(ph["mla_out"], h, attn))
            gates = two_tiles(ph["conv_gate"], h)
            for g in range(LN_AT + 1):
                after = {CENTRE_AT: ((0, total_after(tree_step, 4, tree[:, 0, :])),),
                         LN_AT: ((0, total_after(tree_step, 8, tree[:, 0, :])),)}.get(g, ())
                gates(g, after=after)
            over(pe, LN_AT + 1, KT // 2, gates)
            two_tiles(ph["conv_out"], attn)(0, ready=ln_split)
            over(pe, 1, KT // 2, two_tiles(ph["conv_out"], attn))
            two_tiles(ph["w_out"], merged)(0, ready=merge_split)
            over(pe, 1, KT // 2, two_tiles(ph["w_out"], merged))
            n = 2 * KT + KVT + QT
            two_tiles(ph["ffn2_up"], h)(0, ready=absorbed, base=n - KT,
                                        after=((0, total_after(summed, n, sum_sq[:, :])),))
            over(pe, 1, FT, two_tiles(ph["ffn2_up"], h))
            down(ph["ffn2_down"], hidden, FT)
            pe.wait_ge(summed, n + KT)
            total(sum_sq[:, :])

        @block.vector
        def _(dve):
            def split_unit(phase, g, j):
                n = phase.sizes[j] * P
                dve.wait_ge(hi_ready, SLOTS * (phase.g0 + g) + (j + 1))
                dve.tensor_tensor(w_lo[:, j, 0:n], raw[:, j, 0:n], w_hi[:, j, 0:n], ALU.subtract).then_inc(lo_ready, 1)

            def group(phase, following, work, g, r, i, mid=None, early=None, opening=None):
                def split(j):
                    if not (isinstance(g, int) and g == phase.n - 1):
                        split_unit(phase, g + 1, j)
                    elif following:
                        split_unit(following, 0, j)

                if early:
                    early()
                split(0)
                if opening:
                    opening()
                split(1)
                work(g, 0, r, i)
                split(2)
                if mid:
                    mid(g, r, i)
                split(3)
                work(g, 1, r, i)

            def rounds(phase, following, work, step=1, start=0, mid=None):
                def body(g, r, i):
                    group(phase, following, work, g, r, i, mid)

                over(dve, start, phase.n - 1, body, step)
                body(phase.n - 1, (phase.n - 1) % step, (phase.n - 1) // step)

            def times(dst, src, factor, tile, complete):
                dve.wait_ge(*complete)
                dve.tensor_tensor(dst, src[:, 0:T], factor, ALU.mult).then_inc(tile_read, 1)
                dve.wait_ge(tile_read, tile + 1)

            def after_unit(phase, g, j):
                return unit_used, SLOTS * (phase.g0 + g) + (j + 1)

            def absorb(n, src, g_col, dst, square=True):
                if square:
                    dve.tensor_tensor(sq[:, :], src, src, ALU.mult).then_inc(squared, 1)
                if g_col is not None:
                    dve.tensor_scalar(dst[:, 0:T], src, g_col, None, ALU.mult).then_inc(rounded, 1)
                if g_col is not None:
                    dve.wait_ge(rounded, n + 1)
                    dve.scalar_tensor_tensor(out=dst[:, T:2 * T], in0=src, scalar=g_col, in1=dst[:, 0:T],
                                             op0=ALU.mult, op1=ALU.subtract).then_inc(absorbed, 1)
                dve.wait_ge(squared, n + 1)
                dve.tensor_tensor(sum_sq[:, :], sum_sq[:, :], sq[:, :], ALU.add).then_inc(summed, 1)
                dve.wait_ge(summed, n + 1)

            stats, clears, st = [0], [0], [0]

            def linked(ins):
                st[0] += 1
                ins.then_inc(stat_step, 1)
                dve.wait_ge(stat_step, st[0])

            def clear_sum():
                clears[0] += 1
                dve.memset(sum_sq[:, :], 0.0).then_inc(sums_cleared, 1)
                dve.wait_ge(sums_cleared, clears[0])

            def inverse_root(dst, dim, src=None):
                stats[0] += 1
                n = stats[0]
                src = misc[:, 0:T] if src is None else src
                var, root = (small[:, 0:2], small[:, 2:4]) if n == KV_COL_STAT else (ta[:, :], tb[:, :])
                dve.wait_ge(total_ready, TOTAL_OF_STAT[n])
                dve.tensor_scalar(var, src, 1.0 / dim, EPS, ALU.mult, ALU.add).then_inc(var_ready, 1)
                dve.wait_ge(var_ready, n)
                dve.wait_ge(root_ready, n)
                linked(dve.reciprocal(dst, root))
                linked(dve.tensor_tensor(root, dst, dst, ALU.mult))
                linked(dve.tensor_tensor(root, root, var, ALU.mult))
                linked(dve.tensor_scalar(root, root, -0.5, 1.5, ALU.mult, ALU.add))
                linked(dve.tensor_tensor(dst, dst, root, ALU.mult))

            def factor_of_x():
                inverse_root(rstd[:, :], D)

            dve.wait_ge(gains_loaded, 16)
            for n in range(4):
                for m in range(4 * n, 4 * n + 4):
                    dve.wait_ge(x0_rounded, m + 1)
                    dve.scalar_tensor_tensor(out=h[:, m, T:2 * T], in0=x[:, m, :], scalar=gain["ffn1"][:, m, :],
                                             in1=h[:, m, 0:T], op0=ALU.mult, op1=ALU.subtract).then_inc(x0_split, 1)
                split_unit(phases[0], 0, n)

            def up_work(phase, before):
                def work(g, part, r, i):
                    if part == 0:
                        times(ta[:, :], bank[0], rstd[:, :], g * 2 + phase.t0, after_unit(phase, g, 1))
                        return
                    times(tc[:, :], bank[1], rstd[:, :], g * 2 + (phase.t0 + 1), after_unit(phase, g, 3))
                    dve.wait_ge(gate_active, g + (before + 1))
                    dve.tensor_tensor(prod[:, :], tc[:, :], tb[:, :], ALU.mult).then_inc(hidden_ready, 1)
                    dve.tensor_tensor(hidden[:, g, 0:T], tc[:, :], tb[:, :], ALU.mult).then_inc(hidden_hi, 1)
                    dve.wait_ge(hidden_ready, g + (before + 1))
                    dve.wait_ge(hidden_hi, g + (before + 1))
                    dve.tensor_tensor(hidden[:, g, T:2 * T], prod[:, :], hidden[:, g, 0:T],
                                      ALU.subtract).then_inc(hidden_split, 1)
                return work

            def residual_work(phase, factor, name, absorbed_before, tiles=1):
                def work(g, part, r, i):
                    if tiles == 1 and part == 0:
                        return
                    m = g if tiles == 1 else g * 2 + part
                    b = bank[r if tiles == 1 else part]
                    dve.wait_ge(*after_unit(phase, g, 3 if tiles == 1 else 2 * part + 1))
                    dve.scalar_tensor_tensor(out=x[:, m, :], in0=b[:, 0:T], scalar=factor, in1=x[:, m, :],
                                             op0=ALU.mult, op1=ALU.add).then_inc(tile_read, 1)
                    dve.wait_ge(tile_read, m + (phase.t0 + 1))
                    g_col = None if name is None else gain[name][:, m, :]
                    absorb(m + absorbed_before, x[:, m, :], g_col, h[:, m, :])
                return work

            dve.wait_ge(small_loaded, 3 * 16)
            dve.tensor_copy(pos_f, pos_i[:, :]).then_inc(pos_float, 1)
            phase, work = ph["ffn1_up"], up_work(ph["ffn1_up"], 0)
            group(phase, None, work, 0, 0, 0, opening=factor_of_x)
            rounds(phase, ph["ffn1_down"], work, start=1)
            clear_sum()


            def turns_of_angles(g, r, i):
                dve.wait_ge(pos_spread, 1)
                for n in range(2):
                    dve.tensor_scalar(angle[:, n * T:(n + 1) * T], misc[:, T:2 * T], freq[:, n:n + 1], None,
                                      ALU.mult).then_inc(angle_step, 1)
                dve.wait_ge(angle_step, 2)
                for n, shift in enumerate((0.0, 0.25)):
                    cols = slice(n * T, (n + 1) * T)
                    dve.tensor_scalar(turns[:, cols], angle[:, cols], 1.0 / (2.0 * np.pi), shift,
                                      ALU.mult, ALU.add).then_inc(angle_step, 1)
                dve.wait_ge(angle_step, 4)
                linked(dve.tensor_scalar(turns[:, :], turns[:, :], ROUNDER, ROUNDER, ALU.add, ALU.subtract))

            def reduced_angles(g, r, i):
                src = angle
                for c in TWO_PI_PARTS:
                    linked(dve.scalar_tensor_tensor(out=trig[:, :], in0=turns[:, :], scalar=-c, in1=src[:, :],
                                                    op0=ALU.mult, op1=ALU.add))
                    src = trig
                linked(dve.tensor_scalar(cos, cos, 0.5 * np.pi, None, ALU.add))
                dve.tensor_scalar(trig[:, :], trig[:, :], -PI_BELOW, PI_BELOW, ALU.max, ALU.min).then_inc(angle_ready, 1)

            phase, work = ph["ffn1_down"], residual_work(ph["ffn1_down"], 0.5, "mix", 0)
            group(phase, None, work, 0, 0, 0, mid=turns_of_angles)
            group(phase, None, work, 1, 1, 0, mid=reduced_angles)
            rounds(phase, ph["conv_in"], work, 2, 2)

            def convolve(m, part):
                done = m * (TAPS + 1)
                for t in range(part * TAPS // QUARTERS, (part + 1) * TAPS // QUARTERS):
                    src, weight = padded[:, m, t:t + T], taps[:, m, t:t + 1]
                    acc = conv_acc[:, t % 2 * T:(t % 2 + 1) * T]
                    if t == 0:
                        dve.tensor_scalar(acc, src, weight, taps[:, m, TAPS:TAPS + 1],
                                          ALU.mult, ALU.add).then_inc(tap_done, 1)
                    elif t == 1:
                        dve.tensor_scalar(acc, src, weight, None, ALU.mult).then_inc(tap_done, 1)
                    else:
                        dve.wait_ge(tap_done, done + (t - 1))
                        dve.scalar_tensor_tensor(out=acc, in0=src, scalar=weight, in1=acc,
                                                 op0=ALU.mult, op1=ALU.add).then_inc(tap_done, 1)
                if part == QUARTERS - 1:
                    dve.wait_ge(tap_done, done + TAPS)
                    dve.tensor_tensor(conv[:, m, :], conv_acc[:, 0:T], conv_acc[:, T:2 * T], ALU.add).then_inc(tap_done, 1)

            def conv_in_work(g, part, r, i):
                phase = ph["conv_in"]
                if part == 0:
                    times(ta[:, :], bank[0], rstd[:, :], g * 2 + phase.t0, after_unit(phase, g, 1))
                    return
                times(tc[:, :], bank[1], rstd[:, :], g * 2 + (phase.t0 + 1), after_unit(phase, g, 3))
                dve.wait_ge(glu_open, g + 1)
                dve.tensor_tensor(conv[:, g, :], tc[:, :], tb[:, :], ALU.mult).then_inc(glu_ready, 1)

            def conv_in_mid(g, r, i):
                dve.wait_ge(glu_ready, g)
                if r:
                    convolve(i, r - 1)
                else:
                    convolve(i - 1, QUARTERS - 1)

            def clear_pads():
                dve.memset(padded[:, :, 0:PAD], 0.0).then_inc(pads_cleared, 1)
                dve.memset(padded[:, :, PAD + T:T + 2 * PAD], 0.0).then_inc(pads_cleared, 1)
                dve.wait_ge(pads_cleared, 2)

            group(ph["conv_in"], None, conv_in_work, 0, 0, 0, mid=lambda g, r, i: clear_pads(), opening=factor_of_x)
            rounds(ph["conv_in"], ph["latents"], conv_in_work, QUARTERS, 1, conv_in_mid)

            latents = ph["latents"]
            clear_sum()

            def latent(tile, n, g_col, dst):
                times(tc[:, :], bank[tile % 2], rstd[:, :], latents.t0 + tile,
                      after_unit(latents, tile // 2, 2 * (tile % 2) + 1))
                absorb(KT + n, tc[:, :], g_col, dst, square=False)

            def latents_work(g, part, r, i):
                tile = 2 * g + part
                if g < 2:
                    latent(tile, tile, gain["kv"][:, tile, :], c_kv[:, tile, :])
                elif g == 2:
                    dst = td if part else tc
                    times(dst[:, :], bank[part], rstd[:, :], latents.t0 + tile, after_unit(latents, g, 2 * part + 1))
                    linked(dve.tensor_tensor(dst[:, :], dst[:, :], (sin if part else cos), ALU.mult))
                    if part:
                        linked(dve.tensor_tensor(k_rope[:, :], tc[:, :], td[:, :], ALU.add))
                        inverse_root(rstd_kv[:, :], KV_RANK)
                        inverse_root(rstd_kv_col[:, :], KV_RANK, misc[:, T:T + 2])
                        clear_sum()
                else:
                    n = tile - 6
                    latent(tile, KVT + n, gain["q"][:, n, :], c_q[:, n, :])

            dve.wait_ge(trig_ready, 1)
            for g in range(latents.n):
                mid = None if g else lambda g, r, i: convolve(KT // QUARTERS - 1, QUARTERS - 1)
                group(latents, ph["heads"], latents_work, g, 0, 0, mid=mid)
            inverse_root(rstd_q[:, :], Q_RANK)

            heads = ph["heads"]

            def attend_max(p):
                for j in range(2):
                    dve.wait_ge(scores_ready, p * 2 + (j + 1))
                    dve.tensor_reduce(row_inv[:, j, :], scores[j][:, :].rearrange("p (q k) -> p q k", q=2), AX.X,
                                      ALU.max).then_inc(max_step, 1)
                    dve.wait_ge(max_step, p * 2 + (j + 1))
                    dve.tensor_scalar(row_max[:, j, :], row_inv[:, j, :], -SOFTMAX_SCALE, None,
                                      ALU.mult).then_inc(max_ready, 1)

            def attend_inv(p):
                for j in range(2):
                    dve.wait_ge(exp_ready, p * 4 + (2 * j + 2))
                    dve.reciprocal(row_inv[:, j, :], row_sum[:, j, :]).then_inc(inv_ready, 1)

            def attend_split(p):
                for j in range(2):
                    dve.wait_ge(head_hi, p * 2 + (j + 1))
                    dve.tensor_tensor(attn[:, p * 2 + j, T:2 * T], scores[j][:, 0:T],
                                      attn[:, p * 2 + j, 0:T], ALU.subtract).then_inc(head_split, 1)

            def head_pair(g, r=0, i=0):
                t0 = g * 6 + heads.t0
                first = isinstance(g, int) and g == 0
                last = isinstance(g, int) and g == heads.n - 1
                coming, n = (ph["mla_out"], 0) if last else (heads, g + 1)
                tile = g + KT // QUARTERS
                if not first:
                    attend_max(g - 1)
                convolve(tile, 0)
                if not first:
                    attend_inv(g - 1)
                times(q_nope[:, 0, :], bank[0], rstd_q[:, :], t0, (tile_ready, g * 5 + 1))
                split_unit(coming, n, 0)
                times(rope_raw[:, :], bank[1], rstd_q[:, :], t0 + 1, (tile_ready, g * 5 + 2))
                dve.tensor_tensor(tc[:, :], rope_raw[:, :], cos, ALU.mult).then_inc(head_step, 1)
                times(q_nope[:, 1, :], bank[2], rstd_q[:, :], t0 + 2, after_unit(heads, g, 1))
                split_unit(coming, n, 1)
                convolve(tile, 1)
                times(k_nope[:, 0, :], bank[3], rstd_kv[:, :], t0 + 3, (tile_ready, g * 5 + 3))
                times(k_nope[:, 1, :], bank[0], rstd_kv[:, :], t0 + 4, after_unit(heads, g, 2))
                dve.wait_ge(tile_ready, g * 5 + 4)
                dve.tensor_tensor(td[:, :], bank[1][:, 0:T], sin, ALU.mult).then_inc(tile_read, 1)
                if not first:
                    attend_split(g - 1)
                dve.wait_ge(tile_read, t0 + 6)
                dve.wait_ge(head_step, g * 2 + 1)
                dve.tensor_tensor(q_rope[:, :], tc[:, :], td[:, :], ALU.add).then_inc(head_step, 1)
                split_unit(coming, n, 2)
                convolve(tile, 2)
                convolve(tile, 3)
                split_unit(coming, n, 3)

            head_pair(0)
            over(dve, 1, heads.n - 1, head_pair)
            head_pair(heads.n - 1)

            def mla_out_work(g, part, r, i):
                phase = ph["mla_out"]
                if part == 0:
                    times(ta[:, :], bank[0], rstd[:, :], g * 2 + phase.t0, after_unit(phase, g, 1))
                    return
                dve.wait_ge(mla_open, g + 1)
                times(merged32[:, g, 0:T], bank[1], tb[:, :], g * 2 + (phase.t0 + 1), after_unit(phase, g, 3))

            def mla_out_mid(g, r, i):
                convolve(i + (KT - KT // QUARTERS), r)

            def first_mla_out_mid(g, r, i):
                mla_out_mid(g, r, i)
                attend_split(heads.n - 1)

            def last_softmax():
                attend_max(heads.n - 1)
                attend_inv(heads.n - 1)

            group(ph["mla_out"], None, mla_out_work, 0, 0, 0, mid=first_mla_out_mid, early=last_softmax)
            rounds(ph["mla_out"], ph["conv_gate"], mla_out_work, QUARTERS, 1, mla_out_mid)

            gates = ph["conv_gate"]

            def conv_gate_work(g, part, r=0, i=0):
                m = g * 2 + part
                if not (isinstance(g, int) and g == 0):
                    dve.wait_ge(conv_open, m - 1)
                times((ta, tb)[part][:, :], bank[part], rstd[:, :], m + gates.t0, after_unit(gates, g, 2 * part + 1))

            def add_up(src, before):
                n = KT // 2
                while n:
                    dve.tensor_tensor(tree[:, 0:n, :], src[:, 0:n, :], src[:, n:2 * n, :], ALU.add).then_inc(tree_step, 1)
                    before += 1
                    if n > 1:
                        dve.wait_ge(tree_step, before)
                    src, n = tree, n // 2

            def add_channels(g, r, i):
                dve.wait_ge(tap_done, KT * (TAPS + 1))
                add_up(conv, 0)

            def mean_of_channels():
                dve.wait_ge(total_ready, TOTAL_OF_MEAN)
                dve.tensor_scalar(mean[:, :], misc[:, 0:T], 1.0 / D, None, ALU.mult).then_inc(mean_ready, 1)
                dve.wait_ge(mean_ready, 1)

            def centre(g, r, i):
                for m in range(KT):
                    dve.tensor_tensor(conv[:, m, :], conv[:, m, :], mean[:, :], ALU.subtract).then_inc(centred, 1)

            def add_squares(g, r, i):
                dve.wait_ge(squared_ln, 4)
                add_up(squares, 4)

            def factor_of_channels():
                dve.wait_ge(conv_open, 2 * LN_AT)
                inverse_root(rstd_ln[:, :], D)

            def ln_finish(tile):
                dve.wait_ge(ln_active, tile * 2 + 8)
                products = (tc, td, prod, sq)
                for n in range(4):
                    channels = conv[:, tile + n, :]
                    dve.tensor_tensor(products[n][:, :], ln_gate[n], channels, ALU.mult).then_inc(ln_ready, 1)
                dve.wait_ge(ln_ready, tile + 4)
                for n in range(4):
                    dve.tensor_scalar(attn[:, tile + n, 0:T], products[n][:, :], 1.0, None, ALU.mult).then_inc(ln_hi, 1)
                dve.wait_ge(ln_hi, tile + 4)
                for n in range(4):
                    dve.tensor_tensor(attn[:, tile + n, T:2 * T], products[n][:, :], attn[:, tile + n, 0:T],
                                      ALU.subtract).then_inc(ln_split, 1)

            def ln_mid(g, r=0, i=0):
                tile = g * 4 - 4 * LN_AT
                if not (isinstance(g, int) and g == LN_AT):
                    ln_finish(tile - 4)
                if isinstance(g, int) and g == gates.n - 1:
                    return
                for n in range(4):
                    dve.tensor_tensor(conv[:, tile + n, :], conv[:, tile + n, :], rstd_ln[:, :],
                                      ALU.mult).then_inc(ln_scaled, 1)

            group(gates, None, conv_gate_work, 0, 0, 0, mid=add_channels)
            group(gates, None, conv_gate_work, CENTRE_AT, 0, 0, mid=centre, opening=mean_of_channels)
            group(gates, None, conv_gate_work, CENTRE_AT + 1, 0, 0, mid=add_squares)
            group(gates, None, conv_gate_work, LN_AT, 0, 0, mid=ln_mid, opening=factor_of_channels)
            over(dve, LN_AT + 1, gates.n - 1, lambda g, r, i: group(gates, None, conv_gate_work, g, r, i, mid=ln_mid))
            group(gates, ph["conv_out"], conv_gate_work, gates.n - 1, 0, 0, mid=ln_mid)
            dve.wait_ge(conv_open, KT)

            def conv_out_work(g, part, r, i):
                phase = ph["conv_out"]
                m = g * 2 + part
                times(tb[:, :], bank[part], merged32[:, m, T:2 * T], m + phase.t0,
                      after_unit(phase, g, 2 * part + 1))
                dve.tensor_tensor(tc[:, :], tb[:, :], merged32[:, m, 0:T], ALU.add).then_inc(merge_step, 1)
                dve.tensor_tensor(merged[:, m, 0:T], tb[:, :], merged32[:, m, 0:T], ALU.add).then_inc(merge_hi, 1)
                dve.wait_ge(merge_step, m + 1)
                dve.wait_ge(merge_hi, m + 1)
                dve.tensor_tensor(merged[:, m, T:2 * T], tc[:, :], merged[:, m, 0:T],
                                  ALU.subtract).then_inc(merge_split, 1)

            rounds(ph["conv_out"], ph["w_out"], conv_out_work)
            clear_sum()
            n = KT + KVT + QT
            rounds(ph["w_out"], ph["ffn2_up"], residual_work(ph["w_out"], 1.0, "ffn2", n, 2))
            phase, work = ph["ffn2_up"], up_work(ph["ffn2_up"], FT)
            group(phase, None, work, 0, 0, 0, opening=factor_of_x)
            rounds(phase, ph["ffn2_down"], work, start=1)
            clear_sum()
            rounds(ph["ffn2_down"], None, residual_work(ph["ffn2_down"], 0.5, None, n + KT), 2)
            factor_of_x()
            for m in range(KT):
                dve.scalar_tensor_tensor(out=x[:, m, :], in0=x[:, m, :], scalar=gain["final"][:, m, :],
                                         in1=rstd[:, :], op0=ALU.mult, op1=ALU.mult).then_inc(out_ready, 1)


KV_COL_STAT = 4
TOTAL_OF_STAT = {1: 1, 2: 2, 3: 4, 4: 4, 5: 5, 6: 7, 7: 8, 8: 9}
TOTAL_OF_MEAN = 6
ADDS = 5
CENTRE_AT, LN_AT = 1, 3
QUARTERS = 4
ROUNDER = 1.5 * 2.0 ** 23
PI_BELOW = 3.1415925
TWO_PI_PARTS = (6.25, 17.0 / 512.0, -1.7821788787841797e-05, 3.968374073792802e-09)


def tiled(w):
    k, m = w.shape
    return w.reshape(k // P, P, m // P, P).transpose(2, 0, 1, 3)


def units(tiles, per_unit):
    *lead, n, rows, cols = tiles.shape
    t = tiles.reshape(*lead, n // per_unit, per_unit, rows, cols)
    t = np.swapaxes(t, -3, -2)
    return t.reshape(*lead, n // per_unit, rows, per_unit * cols)


def halves(*columns):
    pair = np.stack([units(c, KT // 2) for c in columns], 1)
    return pair.reshape(-1, P, KT // 2 * P)


def head_stream(w_uq, w_ukv):
    q = w_uq.reshape(QT, P, N_HEADS // 2, 2, HEAD_DIM)
    kv = w_ukv.reshape(KVT, P, N_HEADS // 2, 2, 2 * P)
    q_nope = q[..., :P].transpose(2, 3, 0, 1, 4)
    rope = q[..., P:].transpose(2, 0, 1, 3, 4).reshape(N_HEADS // 2, QT, P, P)
    k_nope = kv[..., :P].transpose(2, 3, 0, 1, 4)
    v = kv[..., P:].transpose(2, 0, 3, 1, 4)
    out = np.zeros((N_HEADS // 2, SLOTS, P, 9 * P), w_uq.dtype)
    join = np.concatenate
    out[:, 0] = units(join([q_nope[:, 0], rope[:, :3]], 1), 9)[:, 0]
    out[:, 1] = units(join([rope[:, 3:], q_nope[:, 1]], 1), 9)[:, 0]
    out[:, 2, :, :8 * P] = units(join([k_nope[:, 0], k_nope[:, 1]], 1), 8)[:, 0]
    out[:, 3, :, :8 * P] = units(v.reshape(N_HEADS // 2, 2 * KVT, P, P), 8)[:, 0]
    return out.reshape(-1, P, 9 * P)


def columns(v):
    return v.reshape(-1, P).T[:, :, None]


def kernel(**inputs):
    import concourse.bacc as _bacc
    from concourse.bass_utils import run_bass_kernel_spmd as _run

    a = {k: np.asarray(v) for k, v in inputs.items()}
    w = {k: v[0] for k, v in a.items() if v.ndim == 3 and k != "x"}
    v = {k: a[k][0] for k in a if a[k].ndim == 2 and k != "positions"}

    cuts = np.cumsum([0, D, D, Q_RANK, KV_RANK, ROPE, D, D])
    conv_a, conv_g, q_down, kv_down, k_rope, gate_conv, gate_mla = (
        w["w_in"][:, lo:hi] for lo, hi in zip(cuts[:-1], cuts[1:]))
    half = ROPE // 2
    swapped = np.concatenate([k_rope[:, half:], k_rope[:, :half]], 1)
    latents = np.concatenate([kv_down, k_rope, k_rope, swapped, swapped, q_down], 1)

    def up(n):
        return halves(tiled(w[f"ffn{n}_w_gate"]), tiled(w[f"ffn{n}_w_up"]))

    def down(n):
        return units(tiled(w[f"ffn{n}_w_down"]), UNIT_MAX).reshape(-1, P, UNIT_MAX * P)

    arrays = {
        "ffn1_up": up(1),
        "ffn1_down": down(1),
        "conv_in": halves(tiled(conv_g), tiled(conv_a)),
        "latents": halves(tiled(latents)),
        "heads": head_stream(w["mla_w_uq"], w["mla_w_ukv"]),
        "mla_out": halves(tiled(gate_mla), tiled(w["mla_w_o"])),
        "conv_gate": halves(tiled(gate_conv)),
        "conv_out": halves(tiled(w["conv_w_pw_out"])),
        "w_out": halves(tiled(w["w_out"])),
        "ffn2_up": up(2),
        "ffn2_down": down(2),
    }
    names = list(arrays)
    arrays["x_in"] = a["x"][0].T.reshape(KT, P, T).transpose(1, 0, 2)
    arrays["pos_in"] = a["positions"]
    arrays["gains_in"] = np.concatenate([columns(g) for g in (
        v["ffn1_norm_g"], v["mix_norm_g"], v["ffn2_norm_g"], a["final_norm_g"], v["conv_ln_g"], v["conv_ln_b"],
        v["mla_q_norm_g"], v["mla_kv_norm_g"])], 1)
    per_channel = np.concatenate([w["conv_w_dw"], a["conv_b_dw"]], 0)
    arrays["conv_in_w"] = per_channel.reshape(TAPS + 1, KT, P).transpose(2, 1, 0)
    eye = np.eye(P, dtype=np.float32)
    arrays["const_in"] = np.concatenate([eye, eye[np.arange(P) ^ half], np.ones((P, P), np.float32)], 1)
    place = np.arange(P) % ROPE
    inverse = 10000.0 ** (-2.0 * (place % half) / ROPE)
    arrays["freq_in"] = np.stack([inverse * np.where(place < half, -1.0, 1.0), inverse], 1).astype(np.float32)

    nc = _bacc.Bacc("TRN2", target_bir_lowering=False, num_devices=1, dynamic_dma_scratch_size=1024)
    handles, feeds = {}, {}
    for name, array in arrays.items():
        array = np.ascontiguousarray(array)
        feeds[f"in_{name}"] = array
        handles[name] = nc.dram_tensor(f"in_{name}", array.shape, mybir.dt.from_np(array.dtype),
                                       kind="ExternalInput").ap()
    out = nc.dram_tensor("out", (P, KT, T), F32, kind="ExternalOutput").ap()
    encoder(nc, {n: handles[n] for n in names}, handles["x_in"], handles["pos_in"], handles["gains_in"],
            handles["conv_in_w"], handles["const_in"], handles["freq_in"], out)
    r = _run(nc, [feeds], core_ids=[0])
    got = r.results[0]["out"]
    return np.ascontiguousarray(got.transpose(2, 1, 0).reshape(1, T, D))
```
